# Optimizing a Trainium2 kernel written in Bass

```python
import jax, jax.numpy as jnp
from jax import lax
import numpy as np

D_MODEL = 2048
BATCH = 1
SEQ = 256
DEPTH = 2

N_MIXERS = 3
EPS = 1e-6
SB_HEADS = 16
SB_HEAD_DIM = D_MODEL // SB_HEADS
SB_BLOCK = 128
GM_WIDTH = D_MODEL
GM_GROUPS = 16
GM_GROUP_DIM = GM_WIDTH // GM_GROUPS
GM_CHUNK = 128
RET_HEADS = 8
RET_QK_DIM = D_MODEL // RET_HEADS
RET_V_DIM = 2 * D_MODEL // RET_HEADS
RET_CHUNK = 128
ROPE_BASE = 10000.0
D_FF = -(-8 * D_MODEL // (3 * 256)) * 256

kernel_name = "hybrid_sb_gmlp_retention_trunk"

def rmsnorm(x, g):
    xf = x.astype(jnp.float32)
    y = xf * lax.rsqrt(jnp.mean(xf * xf, axis=-1, keepdims=True) + EPS)
    return (y * g.astype(jnp.float32)).astype(x.dtype)

def layernorm(x, g):
    xf = x.astype(jnp.float32)
    mu = jnp.mean(xf, axis=-1, keepdims=True)
    xc = xf - mu
    y = xc * lax.rsqrt(jnp.mean(xc * xc, axis=-1, keepdims=True) + EPS)
    return (y * g.astype(jnp.float32)).astype(x.dtype)

def stick_breaking_mixer(h, w_qkv, w_o):
    B, S, D = h.shape
    q, k, v = jnp.split(h @ w_qkv, 3, axis=-1)
    q = q.reshape(B, S, SB_HEADS, SB_HEAD_DIM) * (SB_HEAD_DIM ** -0.5)
    k = k.reshape(B, S, SB_HEADS, SB_HEAD_DIM)
    v = v.reshape(B, S, SB_HEADS, SB_HEAD_DIM)
    nb = S // SB_BLOCK
    qb = q.reshape(B, nb, SB_BLOCK, SB_HEADS, SB_HEAD_DIM).transpose(1, 0, 3, 2, 4)
    key_pos = jnp.arange(S)

    def block(args):
        qi, i = args
        z = jnp.einsum('bhtd,bshd->bhts', qi, k, preferred_element_type=jnp.float32)
        q_pos = i * SB_BLOCK + jnp.arange(SB_BLOCK)
        causal = key_pos[None, :] < q_pos[:, None]
        log_keep = jnp.where(causal, jax.nn.log_sigmoid(-z), 0.0)
        tail = lax.cumsum(log_keep, axis=3, reverse=True) - log_keep
        a = jnp.where(causal, jnp.exp(jax.nn.log_sigmoid(z) + tail), 0.0)
        return jnp.einsum('bhts,bshd->bthd', a.astype(v.dtype), v)

    o = lax.map(block, (qb, jnp.arange(nb)))
    o = o.transpose(1, 0, 2, 3, 4).reshape(B, S, D)
    return o @ w_o

def chunked_gmlp_mixer(h, w_in, v_norm, w_s, b_s, w_o):
    B, S, D = h.shape
    u, v = jnp.split(jax.nn.gelu(h @ w_in), 2, axis=-1)
    v = layernorm(v, v_norm)
    nc = S // GM_CHUNK
    v = v.reshape(B, nc, GM_CHUNK, GM_GROUPS, GM_GROUP_DIM)
    mask = jnp.tril(jnp.ones((GM_CHUNK, GM_CHUNK), dtype=bool))
    ws = jnp.where(mask[None], w_s, 0.0).astype(v.dtype)
    mixed = jnp.einsum('gts,bcsgd->bctgd', ws, v) + b_s.T[None, None, :, :, None]
    return (u * mixed.reshape(B, S, GM_WIDTH)) @ w_o

def rotary(x, pos):
    half = x.shape[-1] // 2
    inv = ROPE_BASE ** (-jnp.linspace(0.0, 1.0, half, dtype=jnp.float32))
    ang = pos.astype(jnp.float32)[:, None] * inv[None, :]
    cos = jnp.cos(ang)[None, :, None, :]
    sin = jnp.sin(ang)[None, :, None, :]
    x1, x2 = x[..., :half], x[..., half:]
    return jnp.concatenate([x1 * cos - x2 * sin, x1 * sin + x2 * cos], axis=-1).astype(x.dtype)

def retention_mixer(h, w_qkvg, gn_gain, w_o):
    B, S, D = h.shape
    q, k, v, g = jnp.split(h @ w_qkvg, [D, 2 * D, 4 * D], axis=-1)
    pos = jnp.arange(S)
    q = rotary(q.reshape(B, S, RET_HEADS, RET_QK_DIM), pos)
    k = rotary(k.reshape(B, S, RET_HEADS, RET_QK_DIM), pos) * (RET_QK_DIM ** -0.5)
    v = v.reshape(B, S, RET_HEADS, RET_V_DIM)
    log_gamma = jnp.log(1.0 - 2.0 ** (-5.0 - jnp.arange(RET_HEADS, dtype=jnp.float32)))
    C = RET_CHUNK
    idx = jnp.arange(C, dtype=jnp.float32)
    diff = idx[:, None] - idx[None, :]
    intra_decay = jnp.where(diff[None] >= 0,
                            jnp.exp(jnp.maximum(diff, 0.0)[None] * log_gamma[:, None, None]), 0.0)
    query_decay = jnp.exp((idx + 1.0)[None, :] * log_gamma[:, None])
    key_decay = jnp.exp((C - 1.0 - idx)[None, :] * log_gamma[:, None])
    chunk_decay = jnp.exp(C * log_gamma)
    nc = S // C

    def to_chunks(t):
        return t.reshape(B, nc, C, RET_HEADS, t.shape[-1]).transpose(1, 0, 3, 2, 4).astype(jnp.float32)

    def step(state, inp):
        qc, kc, vc = inp
        scores = jnp.einsum('bhtk,bhsk->bhts', qc, kc) * intra_decay[None]
        inner = jnp.einsum('bhts,bhsv->bhtv', scores, vc)
        cross = jnp.einsum('bhtk,bhkv->bhtv', qc, state) * query_decay[None, :, :, None]
        new_state = state * chunk_decay[None, :, None, None] + jnp.einsum(
            'bhsk,bhsv->bhkv', kc * key_decay[None, :, :, None], vc)
        return new_state, inner + cross

    state0 = jnp.zeros((B, RET_HEADS, RET_QK_DIM, RET_V_DIM), jnp.float32)
    _, o = lax.scan(step, state0, (to_chunks(q), to_chunks(k), to_chunks(v)))
    o = o.transpose(1, 0, 3, 2, 4).reshape(B, S, RET_HEADS, RET_V_DIM)
    o = rmsnorm(o, gn_gain.reshape(RET_HEADS, RET_V_DIM)).reshape(B, S, 2 * D).astype(h.dtype)
    return (jax.nn.silu(g) * o) @ w_o

def swiglu_ffn(h, w_gate_up, w_down):
    gate, up = jnp.split(h @ w_gate_up, 2, axis=-1)
    return (jax.nn.silu(gate) * up) @ w_down

def setup_inputs(seed: int = 0) -> dict:
    key = jax.random.key(seed)
    ks = jax.random.split(key, 20)
    D, f32 = D_MODEL, jnp.float32
    n_sb = len(range(0, DEPTH, N_MIXERS))
    n_gm = len(range(1, DEPTH, N_MIXERS))
    n_ret = len(range(2, DEPTH, N_MIXERS))

    def w(k, shape, fan_in):
        return jax.random.normal(k, shape, f32) * (fan_in ** -0.5)

    def gain(k, shape):
        return 1.0 + 0.02 * jax.random.normal(k, shape, f32)

    return {
        "x": jax.random.normal(ks[0], (BATCH, SEQ, D), f32),
        "sb_norm": gain(ks[1], (n_sb, D)),
        "sb_w_qkv": w(ks[2], (n_sb, D, 3 * D), D),
        "sb_w_o": w(ks[3], (n_sb, D, D), D),
        "gm_norm": gain(ks[4], (n_gm, D)),
        "gm_w_in": w(ks[5], (n_gm, D, 2 * GM_WIDTH), D),
        "gm_v_norm": gain(ks[6], (n_gm, GM_WIDTH)),
        "gm_w_s": w(ks[7], (n_gm, GM_GROUPS, GM_CHUNK, GM_CHUNK), GM_CHUNK),
        "gm_b_s": 1.0 + 0.1 * jax.random.normal(ks[8], (n_gm, GM_GROUPS, GM_CHUNK), f32),
        "gm_w_o": w(ks[9], (n_gm, GM_WIDTH, D), GM_WIDTH),
        "ret_norm": gain(ks[10], (n_ret, D)),
        "ret_w_qkvg": w(ks[11], (n_ret, D, 6 * D), D),
        "ret_gn": gain(ks[12], (n_ret, 2 * D)),
        "ret_w_o": w(ks[13], (n_ret, 2 * D, D), 2 * D),
        "ffn_norm": gain(ks[14], (DEPTH, D)),
        "ffn_w_gate_up": w(ks[15], (DEPTH, D, 2 * D_FF), D),
        "ffn_w_down": w(ks[16], (DEPTH, D_FF, D), D_FF),
        "final_norm": gain(ks[17], (D,)),
    }

def reference(x, sb_norm, sb_w_qkv, sb_w_o, gm_norm, gm_w_in, gm_v_norm, gm_w_s, gm_b_s, gm_w_o,
              ret_norm, ret_w_qkvg, ret_gn, ret_w_o, ffn_norm, ffn_w_gate_up, ffn_w_down, final_norm):
    h = x
    for i in range(DEPTH):
        kind, j = i % N_MIXERS, i // N_MIXERS
        if kind == 0:
            h = h + stick_breaking_mixer(rmsnorm(h, sb_norm[j]), sb_w_qkv[j], sb_w_o[j])
        elif kind == 1:
            h = h + chunked_gmlp_mixer(rmsnorm(h, gm_norm[j]), gm_w_in[j], gm_v_norm[j],
                                       gm_w_s[j], gm_b_s[j], gm_w_o[j])
        else:
            h = h + retention_mixer(rmsnorm(h, ret_norm[j]), ret_w_qkvg[j], ret_gn[j], ret_w_o[j])
        h = h + swiglu_ffn(rmsnorm(h, ffn_norm[i]), ffn_w_gate_up[i], ffn_w_down[i])
    return rmsnorm(h, final_norm)


_drawn_inputs = setup_inputs


def setup_inputs(seed=0):
    import zlib

    import numpy as np

    out = dict(_drawn_inputs(seed))
    spreads = {}
    factors = {'sb_norm': 3.363,
     'gm_norm': 4.231,
     'gm_v_norm': 24.365,
     'ffn_norm': 3.083,
     'final_norm': 7.972,
     'gm_b_s': 2.741}
    for name, (base, spread) in spreads.items():
        noise = np.random.default_rng([zlib.crc32(name.encode()), seed]).standard_normal(out[name].shape)
        drawn = base * np.exp(spread * noise) if base else spread * noise
        out[name] = __import__('jax').numpy.asarray(drawn.astype(out[name].dtype))
    for name, factor in factors.items():
        out[name] = (out[name] * factor).astype(out[name].dtype)
    return out
```

```python
import concourse.bass as bass
from concourse import mybir
from contextlib import ExitStack


def hybrid_trunk(nc, x, sb_norm, sb_w_qkv, sb_w_o, gm_norm, gm_w_in, gm_v_norm, gm_w_s, gm_b_s, gm_w_o,
                 ffn_norm, ffn_w_gate_up, ffn_w_down, final_norm, out):
    f32 = mybir.dt.float32
    f32r = mybir.dt.float32r
    bf16 = mybir.dt.bfloat16
    ALU = mybir.AluOpType
    ACT = mybir.ActivationFunctionType
    AX = mybir.AxisListType

    P = 128
    S, D = x.shape
    RT = S // P
    F = ffn_w_down.shape[1]
    CH = 512
    KD = D // P
    KF = F // P
    ND = D // CH
    NF = F // CH
    TC = CH // P
    HEADS, DH = 16, D // 16
    HG = TC
    EPS = 1e-6
    SB_SCALE = float(DH) ** -0.5

    RING = 4
    LEAD = 3
    KP = 2
    PD = KD // KP
    PF = KF // KP
    assert PD % RING == 0 and 2 * PF % RING == 0

    AT_QKV = 0
    AT_SBO = AT_QKV + 3 * ND * PD
    AT_UP = [AT_SBO + ND * PD, 0]
    AT_DOWN = [AT_UP[0] + 2 * NF * PD, 0]
    AT_GMI = AT_DOWN[0] + ND * PF
    AT_GMO = AT_GMI + 2 * ND * PD
    AT_UP[1] = AT_GMO + ND * PD
    AT_DOWN[1] = AT_UP[1] + 2 * NF * PD
    PIECES = AT_DOWN[1] + ND * PF

    def half(v):
        return v % 2

    ctx = ExitStack()
    with ctx:
        def sb(name, shape, dt=f32):
            return ctx.enter_context(nc.sbuf_tensor(name, shape, dt))

        def sem(name):
            return ctx.enter_context(nc.semaphore(name))

        h = sb("h", [P, RT, D])
        xT_hi = sb("xT_hi", [P, KD, S], f32r)
        xT_lo = sb("xT_lo", [P, KD, S], f32r)
        raw = sb("raw", [P, RING, KP, CH])
        w_hi = sb("w_hi", [P, RING, KP, CH], f32r)
        w_lo = sb("w_lo", [P, RING, KP, CH], f32r)
        gate = sb("gate", [P, RT, CH])
        res = sb("res", [P, RT, CH])
        gain_bc = sb("gain_bc", [P, D])
        ident = sb("ident", [P, P])
        below = sb("below", [P, P])
        upto = sb("upto", [P, P])
        stop = sb("stop", [P, 3 * P])
        rows = sb("rows", [5 * KD, P])
        cols = sb("cols", [P, 5 * KD])
        junk = sb("junk", [P, RT, CH], bf16)
        sumsq = sb("sumsq", [P, 5, RT, ND])
        total = sb("total", [P, 6, RT])
        rstd = sb("rstd", [P, 6, RT])
        minus_half = sb("minus_half", [P, RT])
        stats = sb("stats", [P, RT, ND, 6])
        moments = sb("moments", [P, RT, 2])

        region = sb("region", [P, 2 * KF * S])
        R0 = nc.lookup_mloc(region).addr
        HB = KF * S * 4

        def at(name, offset, shape, dt=f32):
            return nc.alloc_sbuf_tensor_at(name, shape, dt, offset=R0 + offset)

        hid_hi = at("hid_hi", 0, [P, KF, S], f32r)
        hid_lo = at("hid_lo", HB, [P, KF, S], f32r)
        FREE = KD * S * 4
        CB = RT * CH * 4
        q_s = at("q_s", FREE, [P, RT, CH])
        k_s = at("k_s", FREE + CB, [P, RT, CH])
        v_s = at("v_s", FREE + 2 * CB, [P, RT, CH])
        qT = at("qT", FREE + 3 * CB, [P, HG, S])
        kT = at("kT", FREE + 4 * CB, [P, HG, S])
        ZW = 3 * P
        ZB = ZW * 4
        keep = at("keep", FREE + 5 * CB, [P, ZW])
        take = at("take", FREE + 5 * CB + ZB, [P, ZW])
        prob = at("prob", FREE + 5 * CB + 2 * ZB, [P, ZW])
        probT = at("probT", FREE + 5 * CB + 3 * ZB, [P, ZW])
        left = at("left", FREE + 5 * CB + 4 * ZB, [P, ZW + 2])
        vn = at("vn", HB + FREE, [P, RT, D])
        wsT = at("wsT", HB + FREE + RT * D * 4, [P, KD, P])
        ws_raw = at("ws_raw", FREE, [P, KD, P])
        u_s = at("u_s", FREE + KD * P * 4, [P, RT, CH])
        ws_cur = at("ws_cur", FREE + KD * P * 4 + CB, [P, TC, P])

        acc = ctx.enter_context(nc.psum_tensor("acc", [P, 2 * RT * CH], f32))
        tp = [ctx.enter_context(nc.psum_tensor(f"tp{i}", [P, TC * S], f32)) for i in range(2)]

        raw_loaded = [sem(f"raw_loaded{i}") for i in range(RING)]
        hi_ready, lo_ready, used = sem("hi_ready"), sem("lo_ready"), sem("used")
        consts_step, consts_ready = sem("consts_step"), sem("consts_ready")
        rows_loaded, rows_turned, cols_ready = sem("rows_loaded"), sem("rows_turned"), sem("cols_ready")
        x_loaded = [sem(f"x_loaded{c}") for c in range(ND)]
        n_turned = [sem(f"n{m}_turned") for m in range(4)]
        n_hi = [sem(f"n{m}_hi") for m in range(4)]
        n_lo = [sem(f"n{m}_lo") for m in range(4)]
        n_sq = [sem(f"n{m}_sq") for m in range(5)]
        n_step = [sem(f"n{m}_step") for m in range(6)]
        n_total = [sem(f"n{m}_total") for m in range(6)]
        n_rstd = [sem(f"n{m}_rstd") for m in range(6)]
        q_out, k_out, v_out = sem("q_out"), sem("k_out"), sem("v_out")
        qk_turned, qT_ready, kT_ready = sem("qk_turned"), sem("qT_ready"), sem("kT_ready")
        z_ready, sig_ready = sem("z_ready"), sem("sig_ready")
        scan_ready, prod_ready, prob_ready = sem("scan_ready"), sem("prod_ready"), sem("prob_ready")
        pT_turned, pT_ready = sem("pT_turned"), sem("pT_ready")
        o_ready, o_hi, o_lo = sem("o_ready"), sem("o_hi"), sem("o_lo")
        res_ready = [sem(f"res_ready{i}") for i in range(4)]
        gate_ready = [sem(f"gate_ready{i}") for i in range(2)]
        f_turned = [sem(f"f_turned{i}") for i in range(2)]
        f_hi = [sem(f"f_hi{i}") for i in range(2)]
        f_lo = [sem(f"f_lo{i}") for i in range(2)]
        f_res = [sem(f"f_res{i}") for i in range(2)]
        vgain_loaded, fgain_loaded, ws_loaded = sem("vgain_loaded"), sem("fgain_loaded"), sem("ws_loaded")
        ws_turned, wsT_ready, gelu_ready, stats_ready = (sem("ws_turned"), sem("wsT_ready"), sem("gelu_ready"),
                                                         sem("stats_ready"))
        vn_step, vn_ready, ws_cur_ready, mixed_ready = (sem("vn_step"), sem("vn_ready"), sem("ws_cur_ready"),
                                                        sem("mixed_ready"))
        y_ready, y_turned, y_hi, y_lo = sem("y_ready"), sem("y_turned"), sem("y_hi"), sem("y_lo")
        gained, out_ready, stored = sem("gained"), [sem("out_act"), sem("out_dve")], sem("stored")

        block = ctx.enter_context(nc.Block())

        def fills(base, it, per, p):
            return base // RING + it * (per // RING) + p // RING + 1

        def acc_at(chunk, rt):
            return acc[:, bass.ds(half(chunk) * (RT * CH) + rt * CH, CH)]

        def acc_both(chunk):
            return acc[:, bass.ds(half(chunk) * (RT * CH), RT * CH)].rearrange("p (r n) -> p r n", r=RT)

        def tile(t, k):
            return t[:, bass.ds(k, 1), :].rearrange("p k t -> p (k t)")

        @block.sync
        def _(sp):
            def load(base, it, per, p, src, k0):
                if not (base == 0 and isinstance(it, int) and it == 0 and p < RING):
                    sp.wait_ge(lo_ready, base + it * per + p - RING + 1)
                sp.dma_start(raw[:, p % RING], src[:, k0:k0 + KP, :]).then_inc(raw_loaded[p % RING], 16)

            qkv = sb_w_qkv[0].rearrange("(k p) n -> p k n", p=P)

            def qkv_body(j):
                for sec in range(3):
                    src = qkv[:, :, bass.ds(j * CH + sec * D, CH)]
                    for p in range(PD):
                        load(AT_QKV, j, 3 * PD, sec * PD + p, src, p * KP)

            def square(base, w):
                src = w.rearrange("(k p) n -> p k n", p=P)
                with sp.Fori(0, w.shape[1] // CH) as c:
                    for p in range(PD):
                        load(base, c, PD, p, src[:, :, bass.ds(c * CH, CH)], p * KP)

            def ffn(layer):
                up = ffn_w_gate_up[layer].rearrange("(k p) n -> p k n", p=P)
                with sp.Fori(0, NF) as i:
                    for sec in range(2):
                        src = up[:, :, bass.ds(i * CH + sec * F, CH)]
                        for p in range(PD):
                            load(AT_UP[layer], i, 2 * PD, sec * PD + p, src, p * KP)
                down = ffn_w_down[layer].rearrange("(k p) n -> p k n", p=P)
                with sp.Fori(0, ND // 2) as i:
                    for cc in range(2):
                        src = down[:, :, bass.ds(i * (2 * CH) + cc * CH, CH)]
                        for p in range(PF):
                            load(AT_DOWN[layer], i, 2 * PF, cc * PF + p, src, p * KP)

            qkv_body(0)
            with sp.Fori(1, ND) as j:
                qkv_body(j)
            square(AT_SBO, sb_w_o[0])
            ffn(0)
            w_in = gm_w_in[0].rearrange("(k p) n -> p k n", p=P)
            for sec in range(2):
                with sp.Fori(0, ND) as c:
                    for p in range(PD):
                        load(AT_GMI + sec * ND * PD, c, PD, p, w_in[:, :, bass.ds(c * CH + (1 - sec) * D, CH)], p * KP)
            square(AT_GMO, gm_w_o[0])
            ffn(1)
            o = out.rearrange("(r p) n -> p r n", p=P)
            for c in range(ND):
                sp.wait_ge(out_ready[c % 2], c // 2 + 1)
                sp.dma_start(o[:, :, c * CH:(c + 1) * CH], h[:, :, c * CH:(c + 1) * CH]).then_inc(stored, 16)
            sp.wait_ge(stored, 16 * ND)

        @block.gpsimd
        def _(pool):
            nc.gpsimd.dma_start(gain_bc[:, :], gm_v_norm[0:1, :].to_broadcast([P, D])).then_inc(vgain_loaded, 16)
            for t, v in ((ident[:, :], 0.0), (below[:, :], 1.0), (upto[:, :], 1.0), (stop[:, :], 1.0),
                         (minus_half[:, :], -0.5), (left[:, ZW:ZW + 2], 1.0)):
                nc.gpsimd.memset(t, v).then_inc(consts_step, 1)
            pool.wait_ge(consts_step, 6)

            def select(t, op, fill, base, pattern, mul):
                return nc.gpsimd.affine_select(out=t, in_=t, compare_op=op, fill=fill, base=base, pattern=pattern,
                                               channel_multiplier=mul)

            select(ident[:, :], ALU.not_equal, 1.0, 0, [[-1, P]], 1).then_inc(consts_ready, 1)
            select(below[:, :], ALU.is_gt, 0.0, 0, [[-1, P]], 1).then_inc(consts_ready, 1)
            select(upto[:, :], ALU.is_ge, 0.0, 0, [[1, P]], -1).then_inc(consts_ready, 1)
            select(stop[:, 0:P], ALU.is_ge, 0.0, 0, [[1, P]], -1).then_inc(consts_ready, 1)
            select(stop[:, P:3 * P], ALU.is_ge, 0.0, -P, [[1, 2 * P]], -1).then_inc(consts_ready, 1)

            def power(m):
                pool.wait_ge(n_total[m], 1)
                nc.gpsimd.tensor_tensor(out=rstd[:, m, :], in0=total[:, m, :], in1=minus_half[:, :],
                                        op=ALU.pow).then_inc(n_rstd[m], 1)

            power(0)
            power(1)
            pool.wait_ge(used, AT_GMI)
            nc.gpsimd.dma_start(ws_raw[:, :, :], gm_w_s[0].rearrange("g t s -> t g s")).then_inc(ws_loaded, 16)
            power(2)
            power(5)
            pool.wait_ge(vn_ready, RT)
            nc.gpsimd.dma_start(gain_bc[:, :], final_norm[0:1, :].to_broadcast([P, D])).then_inc(fgain_loaded, 16)
            power(3)
            power(4)

        @block.scalar
        def _(act):
            for m, src in enumerate((sb_norm[0], ffn_norm[0], gm_norm[0], ffn_norm[1])):
                act.dma_start(rows[m * KD:(m + 1) * KD, :], src.rearrange("(k p) -> k p", p=P)).then_inc(rows_loaded, 16)
            act.dma_start(rows[4 * KD:5 * KD, :], gm_b_s[0]).then_inc(rows_loaded, 16)
            for c in range(ND):
                act.dma_start(h[:, :, c * CH:(c + 1) * CH],
                              x[:, c * CH:(c + 1) * CH].rearrange("(r p) n -> p r n", p=P)).then_inc(x_loaded[c], 16)

            def split(base, it, per, p):
                act.wait_ge(raw_loaded[p % RING], 16 * fills(base, it, per, p))
                if not (base == 0 and isinstance(it, int) and it == 0 and p < RING):
                    act.wait_ge(used, base + it * per + p - RING + 1)
                nc.scalar.activation(w_hi[:, p % RING], raw[:, p % RING], ACT.Copy).then_inc(hi_ready, 1)

            def ahead(base, it, per, p):
                if not (base == AT_DOWN[1] and isinstance(it, int) and base + it * per + p + LEAD >= PIECES):
                    split(base, it, per, p + LEAD)

            def turned_gained(m, c, seen):
                act.wait_ge(n_turned[m], seen)
                for k in range(TC):
                    last = nc.scalar.activation(tile(xT_hi, c * TC + k),
                                                tp[0 if m or half(c) == 0 else 1][:, k * S:(k + 1) * S], ACT.Copy,
                                                scale=cols[:, bass.ds(c * TC + (m * KD + k), 1)])
                last.then_inc(n_hi[m], 1)

            def squares(m, c, src):
                for r in range(RT):
                    last = nc.scalar.activation(junk[:, r], src[:, r], ACT.Square,
                                                accum_out=sumsq[:, m, r, bass.ds(c, 1)])
                last.then_inc(n_sq[m], 1)

            def norm_chunk(m, c):
                turned_gained(m, c, c + (2 if m == 2 else 1))
                nc.scalar.activation(h[:, :, bass.ds(c * CH, CH)], res[:, :, :], ACT.Copy)
                squares(m, c, res)

            def q_or_k(j, sec, dst, done, t_end):
                act.wait_ge(used, AT_QKV + j * (3 * PD) + t_end)
                for r in range(RT):
                    last = nc.scalar.activation(dst[:, r], acc_at(j * 3 + sec, r), ACT.Copy, scale=rstd[:, 0, r:r + 1])
                last.then_inc(done, 1)

            def qT_evac(g):
                act.wait_ge(qk_turned, g * 2 + 1)
                nc.scalar.activation(qT[:, :, :], tp[0][:, :].rearrange("p (h t) -> p h t", h=HG),
                                     ACT.Copy).then_inc(qT_ready, 1)

            def sigmoids(g, i):
                act.wait_ge(z_ready, g * HG + (i + 1))
                nc.scalar.activation(keep[:, :], tp[0][:, 0:ZW], ACT.Sigmoid, scale=-SB_SCALE)
                nc.scalar.activation(take[:, :], tp[0][:, 0:ZW], ACT.Sigmoid, scale=SB_SCALE).then_inc(sig_ready, 1)

            def probT_evac(g, i):
                act.wait_ge(pT_turned, g * HG + (i + 1))
                nc.scalar.activation(probT[:, :], tp[0][:, CH:CH + ZW], ACT.Copy).then_inc(pT_ready, 1)

            def o_high(g, i):
                act.wait_ge(o_ready, g * HG + (i + 1))
                nc.scalar.activation(tile(hid_hi, g * HG + i), tp[1][:, (i % 2) * CH:(i % 2) * CH + S],
                                     ACT.Copy).then_inc(o_hi, 1)

            def attention(g, t):
                if t == 1:
                    qT_evac(g)
                for i in range(HG):
                    if t == 9 + 4 * i:
                        o_high(g, i)
                    if t == 7 + 4 * i:
                        probT_evac(g, i)
                for i in range(HG):
                    if t == 5 + 4 * i:
                        sigmoids(g, i)

            for p in range(LEAD):
                split(AT_QKV, 0, 3 * PD, p)
            act.wait_ge(rows_turned, 1)
            nc.scalar.activation(cols[:, :], tp[1][:, 0:5 * KD], ACT.Copy).then_inc(cols_ready, 1)
            act.wait_ge(cols_ready, 1)
            for c in range(ND):
                turned_gained(0, c, c + 1)
            for c in range(ND):
                if c:
                    act.wait_ge(n_sq[0], c)
                squares(0, c, h[:, :, c * CH:(c + 1) * CH])

            def qkv_round(j, with_attention):
                for t in range(3 * PD):
                    ahead(AT_QKV, j, 3 * PD, t)
                    if t == PD - 1:
                        if not with_attention:
                            act.wait_ge(n_rstd[0], 1)
                        q_or_k(j, 0, q_s, q_out, PD)
                    if t == 2 * PD - 1:
                        q_or_k(j, 1, k_s, k_out, 2 * PD)
                    if with_attention:
                        attention(j - 1, t)

            qkv_round(0, False)
            with act.Fori(1, ND) as j:
                qkv_round(j, True)
            g = ND - 1
            for p in range(PD):
                ahead(AT_SBO, 0, PD, p)
                if p == 0:
                    qT_evac(g)
                for i in range(HG):
                    if p == 3 + i:
                        o_high(g, i)
                    if p == 2 + i:
                        probT_evac(g, i)
                for i in range(HG):
                    if p == 1 + i:
                        sigmoids(g, i)

            def residual_rest(m, base):
                with act.Fori(1, ND) as c:
                    for p in range(PD):
                        ahead(base, c, PD, p)
                        if p == 1:
                            norm_chunk(m, c - 1)

            residual_rest(1, AT_SBO)

            def gate_out(layer, i, t_end):
                act.wait_ge(used, AT_UP[layer] + t_end)
                for r in range(RT):
                    last = nc.scalar.activation(gate[:, r], acc_at(0, r), ACT.Silu,
                                                scale=rstd[:, 1 + 2 * layer, r:r + 1])
                last.then_inc(gate_ready[layer], 1)

            def hidden_high(layer, i, turned, seen):
                act.wait_ge(turned, seen)
                nc.scalar.activation(hid_hi[:, bass.ds(i * TC, TC), :],
                                     tp[0][:, :].rearrange("p (k t) -> p k t", k=TC), ACT.Copy).then_inc(f_hi[layer], 1)

            def ffn_up(layer):
                m = 1 + 2 * layer
                for p in range(PD):
                    ahead(AT_UP[layer], 0, PD, p)
                    if p == 1:
                        norm_chunk(m, ND - 1)
                    if p == PD - 1:
                        act.wait_ge(n_rstd[m], 1)
                        gate_out(layer, 0, PD)
                with act.Fori(0, NF - 1) as i:
                    for t in range(2 * PD):
                        ahead(AT_UP[layer] + PD, i, 2 * PD, t)
                        if t == PD + 1:
                            hidden_high(layer, i, f_turned[layer], i + 1)
                        if t == 2 * PD - 1:
                            gate_out(layer, i + 1, PD + i * (2 * PD) + 2 * PD)
                for p in range(PD):
                    ahead(AT_UP[layer] + (2 * NF - 1) * PD, 0, PD, p)

            ffn_up(0)
            for it in range(ND // 2):
                for t in range(2 * PF):
                    ahead(AT_DOWN[0], it, 2 * PF, t)
                    if t == 1 and it == 0:
                        hidden_high(0, NF - 1, n_turned[2], 1)
                    if t == 1 and it > 0:
                        norm_chunk(2, 2 * it - 1)
                    if t == PF + 1:
                        norm_chunk(2, 2 * it)

            def gelu(c, dst):
                act.wait_ge(used, AT_GMI + PD + c * PD)
                for r in range(RT):
                    last = nc.scalar.activation(dst[r], acc_at(c, r), ACT.Gelu_apprx_tanh, scale=rstd[:, 2, r:r + 1])
                last.then_inc(gelu_ready, 1)

            def ws_evac(n):
                act.wait_ge(ws_turned, n + 1)
                nc.scalar.activation(wsT[:, n * 8:(n + 1) * 8, :], tp[1][:, :].rearrange("p (g t) -> p g t", g=8),
                                     ACT.Copy).then_inc(wsT_ready, 1)

            for p in range(PD):
                ahead(AT_GMI, 0, PD, p)
                if p == 1:
                    norm_chunk(2, ND - 1)
                if p == 5:
                    ws_evac(0)
                if p == 7:
                    act.wait_ge(n_rstd[2], 1)
                    gelu(0, [vn[:, r, 0:CH] for r in range(RT)])
                    ws_evac(1)
            with act.Fori(1, ND) as c:
                for p in range(PD):
                    ahead(AT_GMI, c, PD, p)
                    if p == PD - 1:
                        gelu(c, [vn[:, r, bass.ds(c * CH, CH)] for r in range(RT)])

            def y_high(c):
                act.wait_ge(y_turned, c + 1)
                nc.scalar.activation(hid_hi[:, bass.ds(c * TC, TC), :],
                                     tp[0][:, :].rearrange("p (k t) -> p k t", k=TC), ACT.Copy).then_inc(y_hi, 1)

            def u_chunk(c, carried):
                for p in range(PD):
                    ahead(AT_GMI + ND * PD, c, PD, p)
                    if p == 1 and carried:
                        y_high(c - 1)
                    if p == PD - 1:
                        gelu(c + ND, [u_s[:, r] for r in range(RT)])

            u_chunk(0, False)
            with act.Fori(1, ND) as c:
                u_chunk(c, True)
            for p in range(PD):
                ahead(AT_GMO, 0, PD, p)
                if p == 1:
                    y_high(ND - 1)
            residual_rest(3, AT_GMO)
            ffn_up(1)
            hidden_high(1, NF - 1, f_turned[1], NF)

            def final_squares(c):
                act.wait_ge(res_ready[3], c + 2)
                squares(4, c, h[:, :, c * CH:(c + 1) * CH])

            for it in range(ND // 2):
                for t in range(2 * PF):
                    ahead(AT_DOWN[1], it, 2 * PF, t)
                    if t == PF - 1:
                        final_squares(2 * it)
                    if t == 2 * PF - 1:
                        final_squares(2 * it + 1)
            act.wait_ge(n_rstd[4], 1)
            for c in range(0, ND, 2):
                act.wait_ge(gained, c + 1)
                for r in range(RT):
                    last = nc.scalar.activation(h[:, r, c * CH:(c + 1) * CH], h[:, r, c * CH:(c + 1) * CH], ACT.Copy,
                                                scale=rstd[:, 4, r:r + 1])
                last.then_inc(out_ready[0], 1)

        @block.vector
        def _(dve):
            def split(base, it, per, p):
                dve.wait_ge(hi_ready, base + it * per + p + 1)
                nc.vector.tensor_tensor(w_lo[:, p % RING], raw[:, p % RING], w_hi[:, p % RING].bitcast(f32),
                                        ALU.subtract).then_inc(lo_ready, 1)

            def ahead(base, it, per, p):
                if not (base == AT_DOWN[1] and isinstance(it, int) and base + it * per + p + LEAD >= PIECES):
                    split(base, it, per, p + LEAD)

            def gained_low(m, c, seen):
                dve.wait_ge(n_hi[m], seen)
                for k in range(TC):
                    last = nc.vector.scalar_tensor_tensor(
                        out=tile(xT_lo, c * TC + k), in0=tp[0 if m or half(c) == 0 else 1][:, k * S:(k + 1) * S],
                        scalar=cols[:, bass.ds(c * TC + (m * KD + k), 1)], in1=tile(xT_hi, c * TC + k).bitcast(f32),
                        op0=ALU.mult, op1=ALU.subtract)
                last.then_inc(n_lo[m], 1)

            def mean_square(m, seen):
                dve.wait_ge(n_sq[m], seen)
                nc.vector.tensor_reduce(out=total[:, m, :], in_=sumsq[:, m], op=ALU.add, axis=AX.X).then_inc(n_step[m], 1)
                dve.wait_ge(n_step[m], 1)
                nc.vector.tensor_scalar(total[:, m, :], total[:, m, :], 1.0 / D, EPS, ALU.mult,
                                        ALU.add).then_inc(n_total[m], 1)

            def add_residual(which, chunk, seen, dst):
                dve.wait_ge(used, seen)
                nc.vector.tensor_tensor(dst, acc_both(chunk), h[:, :, bass.ds(chunk * CH, CH)],
                                        ALU.add).then_inc(res_ready[which], 1)

            def v_evac(j):
                dve.wait_ge(used, AT_QKV + j * (3 * PD) + 3 * PD)
                for r in range(RT):
                    last = nc.vector.tensor_scalar(v_s[:, r], acc_at(j * 3 + 2, r), rstd[:, 0, r:r + 1], None, ALU.mult)
                last.then_inc(v_out, 1)

            def kT_evac(g):
                dve.wait_ge(qk_turned, g * 2 + 2)
                nc.vector.tensor_copy(kT[:, :, :], tp[1][:, :].rearrange("p (h t) -> p h t", h=HG)).then_inc(kT_ready, 1)

            def break_stick(g, i):
                n = g * HG + (i + 1)
                dve.wait_ge(sig_ready, n)
                nc.vector.tensor_tensor_scan(left[:, ZW - 1::-1], keep[:, ZW - 1::-1], stop[:, ZW - 1::-1], 1.0,
                                             ALU.mult, ALU.max).then_inc(scan_ready, 1)
                dve.wait_ge(scan_ready, n)
                nc.vector.tensor_tensor(prob[:, :], take[:, :], left[:, 1:ZW + 1], ALU.mult).then_inc(prod_ready, 1)
                dve.wait_ge(prod_ready, n)
                for b in (0, 2):
                    last = nc.vector.tensor_tensor(prob[:, b * P:(b + 1) * P], prob[:, b * P:(b + 1) * P], below[:, :],
                                                   ALU.mult)
                last.then_inc(prob_ready, 1)

            def o_low(g, i):
                dve.wait_ge(o_hi, g * HG + (i + 1))
                nc.vector.tensor_tensor(tile(hid_lo, g * HG + i), tp[1][:, (i % 2) * CH:(i % 2) * CH + S],
                                        tile(hid_hi, g * HG + i).bitcast(f32), ALU.subtract).then_inc(o_lo, 1)

            def attention(g, t):
                if t == 3:
                    kT_evac(g)
                for i in range(HG):
                    if t == 9 + 4 * i:
                        o_low(g, i)
                for i in range(HG):
                    if t == 5 + 4 * i:
                        break_stick(g, i)

            for p in range(LEAD):
                split(AT_QKV, 0, 3 * PD, p)
            dve.wait_ge(cols_ready, 1)
            for c in range(ND):
                gained_low(0, c, c + 1)
            dve.wait_ge(consts_ready, 5)

            def qkv_round(j, with_attention):
                for t in range(3 * PD):
                    ahead(AT_QKV, j, 3 * PD, t)
                    if t == 1 and not with_attention:
                        mean_square(0, ND)
                    if with_attention:
                        attention(j - 1, t)
                    if t == 3 * PD - 1:
                        if not with_attention:
                            dve.wait_ge(n_rstd[0], 1)
                        v_evac(j)

            qkv_round(0, False)
            with dve.Fori(1, ND) as j:
                qkv_round(j, True)
            g = ND - 1
            for p in range(PD):
                ahead(AT_SBO, 0, PD, p)
                if p == 0:
                    kT_evac(g)
                for i in range(HG):
                    if p == 3 + i:
                        o_low(g, i)
                for i in range(HG):
                    if p == 1 + i:
                        break_stick(g, i)
                if p == PD - 1:
                    add_residual(0, 0, AT_SBO + PD, res[:, :, :])

            def residual_rest(which, m, base):
                with dve.Fori(1, ND) as c:
                    for p in range(PD):
                        ahead(base, c, PD, p)
                        if p == 1:
                            gained_low(m, c - 1, c)
                        if p == PD - 1:
                            dve.wait_ge(n_sq[m], c)
                            add_residual(which, c, base + PD + c * PD, res[:, :, :])

            residual_rest(0, 1, AT_SBO)

            def up_out(layer, t_end, i, done):
                dve.wait_ge(used, AT_UP[layer] + t_end)
                dve.wait_ge(gate_ready[layer], i + 1)
                for r in range(RT):
                    last = nc.vector.scalar_tensor_tensor(out=res[:, r], in0=acc_at(1, r),
                                                          scalar=rstd[:, 1 + 2 * layer, r:r + 1], in1=gate[:, r],
                                                          op0=ALU.mult, op1=ALU.mult)
                last.then_inc(done, 1)

            def hidden_low(layer, i, done):
                dve.wait_ge(f_hi[layer], i + 1)
                ks = bass.ds(i * TC, TC)
                nc.vector.tensor_tensor(hid_lo[:, ks, :], tp[0][:, :].rearrange("p (k t) -> p k t", k=TC),
                                        hid_hi[:, ks, :].bitcast(f32), ALU.subtract).then_inc(done, 1)

            def ffn_up(layer):
                m = 1 + 2 * layer
                for p in range(PD):
                    ahead(AT_UP[layer], 0, PD, p)
                    if p == 1:
                        gained_low(m, ND - 1, ND)
                    if p == 2:
                        mean_square(m, ND)
                        dve.wait_ge(n_rstd[m], 1)
                with dve.Fori(0, NF - 1) as i:
                    for t in range(2 * PD):
                        ahead(AT_UP[layer] + PD, i, 2 * PD, t)
                        if t == PD - 1:
                            up_out(layer, i * (2 * PD) + 2 * PD, i, f_res[layer])
                        if t == PD + 1:
                            hidden_low(layer, i, f_lo[layer])
                for p in range(PD):
                    ahead(AT_UP[layer] + (2 * NF - 1) * PD, 0, PD, p)
                up_out(layer, 2 * NF * PD, NF - 1, f_res[1] if layer else res_ready[1])

            ffn_up(0)
            for it in range(ND // 2):
                for t in range(2 * PF):
                    c = 2 * it + t // PF
                    ahead(AT_DOWN[0], it, 2 * PF, t)
                    if t == 1 and it == 0:
                        hidden_low(0, NF - 1, f_lo[0])
                    elif t % PF == 1:
                        gained_low(2, c - 1, c)
                    if t % PF == PF - 1:
                        if c:
                            dve.wait_ge(n_sq[2], c)
                        add_residual(1, c, AT_DOWN[0] + (c + 1) * PF, res[:, :, :])

            def v_stats(c):
                dve.wait_ge(gelu_ready, c + 1)
                for r in range(RT):
                    last = nc.vector.bn_stats(tile(stats[:, r], c), vn[:, r, bass.ds(c * CH, CH)])
                last.then_inc(stats_ready, 1)

            for p in range(PD):
                ahead(AT_GMI, 0, PD, p)
                if p == 1:
                    gained_low(2, ND - 1, ND)
                if p == 2:
                    mean_square(2, ND)
                if p == PD - 1:
                    v_stats(0)
            with dve.Fori(1, ND) as c:
                for p in range(PD):
                    ahead(AT_GMI, c, PD, p)
                    if p == PD - 1:
                        v_stats(c)

            def norm_v(r):
                dve.wait_ge(n_rstd[5], 1)
                nc.vector.tensor_scalar(vn[:, r], vn[:, r], moments[:, r, 0:1], rstd[:, 5, r:r + 1], ALU.subtract,
                                        ALU.mult).then_inc(vn_step, 1)
                dve.wait_ge(vn_step, r + 1)
                nc.vector.tensor_tensor(vn[:, r], vn[:, r], gain_bc[:, :], ALU.mult).then_inc(vn_ready, 1)

            def ws_mask(c):
                for g in range(TC):
                    last = nc.vector.tensor_tensor(ws_cur[:, g], tile(wsT, c * TC + g), upto[:, :], ALU.mult)
                last.then_inc(ws_cur_ready, 1)

            def gated(c):
                dve.wait_ge(mixed_ready, c + 1)
                dve.wait_ge(gelu_ready, c + (ND + 1))
                for r in range(RT):
                    for g in range(TC):
                        cs = slice(g * P, (g + 1) * P)
                        last = nc.vector.scalar_tensor_tensor(
                            out=res[:, r, cs], in0=tp[1][:, r * CH + g * P:r * CH + (g + 1) * P],
                            scalar=cols[:, bass.ds(c * TC + (4 * KD + g), 1)], in1=u_s[:, r, cs],
                            op0=ALU.add, op1=ALU.mult)
                last.then_inc(y_ready, 1)

            def y_low(c):
                dve.wait_ge(y_hi, c + 1)
                ks = bass.ds(c * TC, TC)
                nc.vector.tensor_tensor(hid_lo[:, ks, :], tp[0][:, :].rearrange("p (k t) -> p k t", k=TC),
                                        hid_hi[:, ks, :].bitcast(f32), ALU.subtract).then_inc(y_lo, 1)

            dve.wait_ge(stats_ready, ND)
            for r in range(RT):
                last = nc.vector.bn_aggr(moments[:, r], stats[:, r].rearrange("p c s -> p (c s)"))
            last.then_inc(n_step[5], 1)
            dve.wait_ge(n_step[5], 1)
            nc.vector.tensor_scalar(total[:, 5, :], moments[:, :, 1], EPS, None, ALU.add).then_inc(n_total[5], 1)
            for p in range(PD):
                ahead(AT_GMI + ND * PD, 0, PD, p)
                if p == 1:
                    dve.wait_ge(wsT_ready, 2)
                    ws_mask(0)
                    dve.wait_ge(vgain_loaded, 16)
                    norm_v(0)
                if p == 3:
                    norm_v(1)
                if p == PD - 1:
                    gated(0)
            with dve.Fori(1, ND) as c:
                for p in range(PD):
                    ahead(AT_GMI + ND * PD, c, PD, p)
                    if p == 0:
                        ws_mask(c)
                    if p == 1:
                        y_low(c - 1)
                    if p == PD - 1:
                        gated(c)
            for p in range(PD):
                ahead(AT_GMO, 0, PD, p)
                if p == 1:
                    y_low(ND - 1)
                if p == PD - 1:
                    add_residual(2, 0, AT_GMO + PD, res[:, :, :])
            residual_rest(2, 3, AT_GMO)
            ffn_up(1)
            hidden_low(1, NF - 1, res_ready[3])
            dve.wait_ge(fgain_loaded, 16)

            def gain_final(c):
                dve.wait_ge(n_sq[4], c + 1)
                for r in range(RT):
                    last = nc.vector.tensor_tensor(h[:, r, c * CH:(c + 1) * CH], h[:, r, c * CH:(c + 1) * CH],
                                                   gain_bc[:, c * CH:(c + 1) * CH], ALU.mult)
                last.then_inc(gained, 1)

            for it in range(ND // 2):
                for t in range(2 * PF):
                    c = 2 * it + t // PF
                    ahead(AT_DOWN[1], it, 2 * PF, t)
                    if t % PF == 1 and c:
                        gain_final(c - 1)
                    if t % PF == PF - 1:
                        add_residual(3, c, AT_DOWN[1] + (c + 1) * PF, h[:, :, c * CH:(c + 1) * CH])
            mean_square(4, ND)
            gain_final(ND - 1)
            dve.wait_ge(n_rstd[4], 1)
            dve.wait_ge(gained, ND)
            for c in range(1, ND, 2):
                for r in range(RT):
                    last = nc.vector.tensor_scalar(h[:, r, c * CH:(c + 1) * CH], h[:, r, c * CH:(c + 1) * CH],
                                                   rstd[:, 4, r:r + 1], None, ALU.mult)
                last.then_inc(out_ready[1], 1)

        @block.tensor
        def _(pe):
            def piece(base, it, per, p, chunk, k0, K, hi, lo):
                pe.wait_ge(lo_ready, base + it * per + p + 1)
                for k in range(KP):
                    kt = k0 + k
                    for r in range(RT):
                        rs = slice(r * P, (r + 1) * P)
                        dst = acc_at(chunk, r)
                        nc.tensor.matmul(dst, hi[:, kt, rs], w_hi[:, p % RING, k], start=(kt == 0), stop=False)
                        nc.tensor.matmul(dst, hi[:, kt, rs], w_lo[:, p % RING, k], start=False, stop=False)
                        last = nc.tensor.matmul(dst, lo[:, kt, rs], w_hi[:, p % RING, k], start=False,
                                                stop=(kt == K - 1))
                last.then_inc(used, 1)

            def turn(dst, src):
                for k in range(TC):
                    for r in range(RT):
                        last = nc.tensor.transpose(dst[:, k * S + r * P:k * S + (r + 1) * P],
                                                   src[:, r, k * P:(k + 1) * P], ident[:, :])
                return last

            pe.wait_ge(consts_ready, 5)
            pe.wait_ge(rows_loaded, 5 * 16)
            nc.tensor.transpose(tp[1][:, 0:5 * KD], rows[:, :], ident[0:5 * KD, 0:5 * KD]).then_inc(rows_turned, 1)

            def turn_x(c):
                pe.wait_ge(x_loaded[c], 16)
                if c == 1:
                    pe.wait_ge(cols_ready, 1)
                if c >= 2:
                    pe.wait_ge(n_lo[0], c - 1)
                turn(tp[c % 2], h[:, :, c * CH:(c + 1) * CH]).then_inc(n_turned[0], 1)

            def turn_qk(g, second):
                if not second:
                    pe.wait_ge(q_out, g + 1)
                    pe.wait_ge(k_out, g + 1)
                    pe.wait_ge(v_out, g + 1)
                turn(tp[second], k_s if second else q_s).then_inc(qk_turned, 1)

            def scores(g, i):
                if i == 0:
                    pe.wait_ge(qT_ready, g + 1)
                    pe.wait_ge(kT_ready, g + 1)
                else:
                    pe.wait_ge(sig_ready, g * HG + i)
                nc.tensor.matmul(tp[0][:, 0:P], qT[:, i, 0:P], kT[:, i, 0:P], start=True, stop=True)
                nc.tensor.matmul(tp[0][:, P:3 * P], qT[:, i, P:2 * P], kT[:, i, :], start=True,
                                 stop=True).then_inc(z_ready, 1)

            def turn_prob(g, i):
                pe.wait_ge(prob_ready, g * HG + (i + 1))
                if i:
                    pe.wait_ge(pT_ready, g * HG + i)
                for b in range(3):
                    last = nc.tensor.transpose(tp[0][:, CH + b * P:CH + (b + 1) * P], prob[:, b * P:(b + 1) * P],
                                               ident[:, :])
                last.then_inc(pT_turned, 1)

            def values(g, i):
                pe.wait_ge(pT_ready, g * HG + (i + 1))
                if i >= 2:
                    pe.wait_ge(o_lo, g * HG + (i - 1))
                o = tp[1][:, (i % 2) * CH:(i % 2) * CH + S]
                hs = slice(i * P, (i + 1) * P)
                nc.tensor.matmul(o, v_s[:, 0, hs], probT[:, 0:2 * P], start=True, stop=False)
                nc.tensor.matmul(o[:, P:2 * P], v_s[:, 1, hs], probT[:, 2 * P:3 * P], start=False,
                                 stop=True).then_inc(o_ready, 1)

            def attention(g, t):
                if t == 1:
                    turn_qk(g, 0)
                if t == 3:
                    turn_qk(g, 1)
                for i in range(HG):
                    if t == 9 + 4 * i:
                        values(g, i)
                    if t == 7 + 4 * i:
                        turn_prob(g, i)
                for i in range(HG):
                    if t == 5 + 4 * i:
                        scores(g, i)

            def qkv_round(j, with_attention):
                for sec in range(3):
                    for p in range(PD):
                        t = sec * PD + p
                        if p == 0 and (with_attention or sec == 2):
                            pe.wait_ge((k_out, v_out, q_out)[sec], j + (1 if sec == 2 else 0))
                        if not with_attention and sec == 0:
                            pe.wait_ge(n_lo[0], p * KP // TC + 1)
                        piece(AT_QKV, j, 3 * PD, t, j * 3 + sec, p * KP, KD, xT_hi, xT_lo)
                        if not with_attention and t in (0, 2):
                            turn_x(2 + t // 2)
                        if with_attention:
                            attention(j - 1, t)

            turn_x(0)
            turn_x(1)
            qkv_round(0, False)
            with pe.Fori(1, ND) as j:
                qkv_round(j, True)

            g = ND - 1
            pe.wait_ge(k_out, ND)
            for p in range(PD):
                if p * KP >= (ND - 1) * TC:
                    pe.wait_ge(o_lo, p * KP + KP)
                elif p == 0:
                    pe.wait_ge(o_lo, (ND - 1) * HG)
                piece(AT_SBO, 0, PD, p, 0, p * KP, KD, hid_hi, hid_lo)
                if p == 0:
                    turn_qk(g, 0)
                    turn_qk(g, 1)
                for i in range(HG):
                    if p == 3 + i:
                        values(g, i)
                    if p == 2 + i:
                        turn_prob(g, i)
                for i in range(HG):
                    if p == 1 + i:
                        scores(g, i)

            def residual_rest(which, m, base, hi, lo):
                with pe.Fori(1, ND) as c:
                    for p in range(PD):
                        piece(base, c, PD, p, c, p * KP, KD, hi, lo)
                        if p == 1:
                            pe.wait_ge(res_ready[which], c)
                            turn(tp[0], res).then_inc(n_turned[m], 1)

            pe.wait_ge(v_out, ND)
            residual_rest(0, 1, AT_SBO, hid_hi, hid_lo)

            def ffn_up(layer, which):
                m = 1 + 2 * layer
                base = AT_UP[layer]
                for p in range(PD):
                    if p == 0:
                        pe.wait_ge(n_lo[m], ND - 1)
                    if p * KP == (ND - 1) * TC:
                        pe.wait_ge(n_lo[m], ND)
                    piece(base, 0, PD, p, 0, p * KP, KD, xT_hi, xT_lo)
                    if p == 1:
                        pe.wait_ge(res_ready[which], ND)
                        turn(tp[0], res).then_inc(n_turned[m], 1)

                with pe.Fori(0, NF - 1) as i:
                    for p in range(PD):
                        piece(base + PD, i, 2 * PD, p, 1, p * KP, KD, xT_hi, xT_lo)
                    pe.wait_ge(gate_ready[layer], i + 1)
                    for p in range(PD):
                        piece(base + PD, i, 2 * PD, PD + p, 0, p * KP, KD, xT_hi, xT_lo)
                        if p == 1:
                            pe.wait_ge(f_res[layer], i + 1)
                            turn(tp[0], res).then_inc(f_turned[layer], 1)
                for p in range(PD):
                    piece(base + (2 * NF - 1) * PD, 0, PD, p, 1, p * KP, KD, xT_hi, xT_lo)
                pe.wait_ge(gate_ready[layer], NF)

            ffn_up(0, 0)
            pe.wait_ge(f_lo[0], NF - 1)
            with pe.Fori(0, ND // 2) as it:
                for t in range(2 * PF):
                    p = t % PF
                    if t == PF - 2:
                        pe.wait_ge(f_lo[0], NF)
                    piece(AT_DOWN[0], it, 2 * PF, t, t // PF, p * KP, KF, hid_hi, hid_lo)
                    if t == 1:
                        pe.wait_ge(res_ready[1], it * 2 + 1)
                        turn(tp[0], res).then_inc(n_turned[2], 1)
                    if t == PF + 1:
                        pe.wait_ge(res_ready[1], it * 2 + 2)
                        turn(tp[0], res).then_inc(n_turned[2], 1)

            for p in range(PD):
                if p == 0:
                    pe.wait_ge(n_lo[2], ND - 1)
                if p * KP == (ND - 1) * TC:
                    pe.wait_ge(n_lo[2], ND)
                piece(AT_GMI, 0, PD, p, 0, p * KP, KD, xT_hi, xT_lo)
                if p == 1:
                    pe.wait_ge(res_ready[1], ND + 1)
                    turn(tp[0], res).then_inc(n_turned[2], 1)
                if p in (5, 7):
                    n = (p - 5) // 2
                    pe.wait_ge(ws_loaded, 16)
                    if n:
                        pe.wait_ge(wsT_ready, 1)
                    for g in range(8):
                        last = nc.tensor.transpose(tp[1][:, g * P:(g + 1) * P], ws_raw[:, n * 8 + g, :], ident[:, :])
                    last.then_inc(ws_turned, 1)
            for p in range(PD):
                piece(AT_GMI + PD, 0, PD, p, 1, p * KP, KD, xT_hi, xT_lo)
            with pe.Fori(2, ND) as c:
                pe.wait_ge(gelu_ready, c - 1)
                for p in range(PD):
                    piece(AT_GMI, c, PD, p, c, p * KP, KD, xT_hi, xT_lo)

            def u_chunk(c, carried):
                pe.wait_ge(gelu_ready, c + (ND - 1))
                for p in range(PD):
                    piece(AT_GMI + ND * PD, c, PD, p, c, p * KP, KD, xT_hi, xT_lo)
                    if p == 1 and carried:
                        pe.wait_ge(y_ready, c)
                        turn(tp[0], res).then_inc(y_turned, 1)
                    if p == 6:
                        pe.wait_ge(ws_cur_ready, c + 1)
                        if not carried:
                            pe.wait_ge(vn_ready, RT)
                        for r in range(RT):
                            for g in range(TC):
                                last = nc.tensor.matmul(tp[1][:, r * CH + g * P:r * CH + (g + 1) * P], ws_cur[:, g],
                                                        vn[:, r, bass.ds(c * CH + g * P, P)], start=True, stop=True)
                        last.then_inc(mixed_ready, 1)

            u_chunk(0, False)
            with pe.Fori(1, ND) as c:
                u_chunk(c, True)
            pe.wait_ge(gelu_ready, 2 * ND - 1)
            for p in range(PD):
                if p == 0:
                    pe.wait_ge(y_lo, ND - 1)
                if p * KP == (ND - 1) * TC:
                    pe.wait_ge(y_lo, ND)
                piece(AT_GMO, 0, PD, p, 0, p * KP, KD, hid_hi, hid_lo)
                if p == 1:
                    pe.wait_ge(y_ready, ND)
                    turn(tp[0], res).then_inc(y_turned, 1)
            pe.wait_ge(gelu_ready, 2 * ND)
            residual_rest(2, 3, AT_GMO, hid_hi, hid_lo)
            ffn_up(1, 2)
            pe.wait_ge(f_res[1], NF)
            turn(tp[0], res).then_inc(f_turned[1], 1)
            pe.wait_ge(f_lo[1], NF - 1)
            with pe.Fori(0, ND // 2) as it:
                for t in range(2 * PF):
                    p = t % PF
                    if t == PF - 2:
                        pe.wait_ge(res_ready[3], 1)
                    if t == PF:
                        pe.wait_ge(res_ready[3], it * 2 + 1)
                    piece(AT_DOWN[1], it, 2 * PF, t, t // PF, p * KP, KF, hid_hi, hid_lo)
                    if t == PF + 2:
                        pe.wait_ge(res_ready[3], it * 2 + 2)


_INS = ["x", "sb_norm", "sb_w_qkv", "sb_w_o", "gm_norm", "gm_w_in", "gm_v_norm", "gm_w_s", "gm_b_s", "gm_w_o",
        "ffn_norm", "ffn_w_gate_up", "ffn_w_down", "final_norm"]


def kernel(**inputs):
    import numpy as _np
    import concourse.bacc as _bacc
    from concourse import mybir as _mybir
    from concourse.bass_utils import run_bass_kernel_spmd as _run

    nc = _bacc.Bacc("TRN2", target_bir_lowering=False, num_devices=1)
    arrays, args = {}, []
    for name in _INS:
        a = _np.ascontiguousarray(inputs[name])
        if name == "x":
            a = a.reshape(a.shape[1:])
        if name == "final_norm":
            a = a.reshape(1, -1)
        arrays[f"in_{name}"] = a
        args.append(nc.dram_tensor(f"in_{name}", a.shape, _mybir.dt.from_np(a.dtype), kind="ExternalInput").ap())
    rows, width = arrays["in_x"].shape
    out = nc.dram_tensor("out_0", (rows, width), _mybir.dt.float32, kind="ExternalOutput").ap()
    hybrid_trunk(nc, *args, out)
    r = _run(nc, [arrays], core_ids=[0])
    return r.results[0]["out_0"].reshape(1, rows, width)
```

```python
import concourse.bass as bass
from concourse import mybir
from contextlib import ExitStack


def hybrid_trunk(nc, x, sb_norm, sb_w_qkv, sb_w_o, gm_norm, gm_w_in, gm_v_norm, gm_w_s, gm_b_s, gm_w_o,
                 ffn_norm, ffn_w_gate_up, ffn_w_down, final_norm, out):
    f32 = mybir.dt.float32
    f32r = mybir.dt.float32r
    bf16 = mybir.dt.bfloat16
    ALU = mybir.AluOpType
    ACT = mybir.ActivationFunctionType
    AX = mybir.AxisListType

    P = 128
    S, D = x.shape
    RT = S // P
    F = ffn_w_down.shape[1]
    CH = 512
    KD = D // P
    KF = F // P
    ND = D // CH
    NF = F // CH
    TC = CH // P
    HEADS, DH = 16, D // 16
    HG = TC
    EPS = 1e-6
    SB_SCALE = float(DH) ** -0.5

    RING = 4
    LEAD = 3
    KP = 2
    PD = KD // KP
    PF = KF // KP
    assert PD % RING == 0 and 2 * PF % RING == 0

    AT_QKV = 0
    AT_SBO = AT_QKV + 3 * ND * PD
    AT_UP = [AT_SBO + ND * PD, 0]
    AT_DOWN = [AT_UP[0] + 2 * NF * PD, 0]
    AT_GMI = AT_DOWN[0] + ND * PF
    AT_GMO = AT_GMI + 2 * ND * PD
    AT_UP[1] = AT_GMO + ND * PD
    AT_DOWN[1] = AT_UP[1] + 2 * NF * PD
    PIECES = AT_DOWN[1] + ND * PF

    def half(v):
        return v % 2

    ctx = ExitStack()
    with ctx:
        def sb(name, shape, dt=f32):
            return ctx.enter_context(nc.sbuf_tensor(name, shape, dt))

        def sem(name):
            return ctx.enter_context(nc.semaphore(name))

        h = sb("h", [P, RT, D])
        xT = sb("xT", [P, KD, 2, S], f32r)
        xT_hi, xT_lo = xT[:, :, 0], xT[:, :, 1]
        raw = sb("raw", [P, RING, KP, CH])
        w_hi = sb("w_hi", [P, RING, KP, CH], f32r)
        w_lo = sb("w_lo", [P, RING, KP, CH], f32r)
        gate = sb("gate", [P, TC, S])
        res = sb("res", [P, RT, CH])
        hidden = res[:, :, :].rearrange("p r (k t) -> p (r k) t", t=S)
        spread = gate[:, 0].rearrange("p (r t) -> p r t", r=RT)
        rstd_row = sb("rstd_row", [P, S])
        gain_bc = sb("gain_bc", [P, D])
        ident = sb("ident", [P, P])
        below = sb("below", [P, P])
        upto = sb("upto", [P, P])
        stop = sb("stop", [P, 3 * P])
        rows_first = sb("rows_first", [KD, P])
        rows = sb("rows", [4 * KD, P])
        cols = sb("cols", [P, 5 * KD])
        junk = sb("junk", [P, RT, CH], bf16)
        sumsq = sb("sumsq", [P, 5, RT, ND])
        total = sb("total", [P, 6, RT])
        rstd = sb("rstd", [P, 6, RT])
        minus_half = sb("minus_half", [P, RT])
        stats = sb("stats", [P, RT, ND, 6])
        moments = sb("moments", [P, RT, 2])

        region = sb("region", [P, 2 * KF * S])
        R0 = nc.lookup_mloc(region).addr
        HB = KF * S * 4

        def at(name, offset, shape, dt=f32):
            return nc.alloc_sbuf_tensor_at(name, shape, dt, offset=R0 + offset)

        hid_hi = at("hid_hi", 0, [P, KF, S], f32r)
        hid_lo = at("hid_lo", HB, [P, KF, S], f32r)
        FREE = KD * S * 4
        CB = RT * CH * 4
        q_s = at("q_s", FREE, [P, RT, CH])
        k_s = at("k_s", FREE + CB, [P, RT, CH])
        v_hi = at("v_hi", FREE + 2 * CB, [P, RT, CH], f32r)
        qT_hi = at("qT_hi", FREE + 3 * CB, [P, HG, S], f32r)
        kT_hi = at("kT_hi", FREE + 4 * CB, [P, HG, S], f32r)
        v_lo = at("v_lo", HB + FREE + 2 * CB, [P, RT, CH], f32r)
        qT_lo = at("qT_lo", HB + FREE + 3 * CB, [P, HG, S], f32r)
        kT_lo = at("kT_lo", HB + FREE + 4 * CB, [P, HG, S], f32r)
        ZW = 3 * P
        ZB = ZW * 4
        keep = at("keep", FREE + 5 * CB, [P, ZW])
        take = at("take", FREE + 5 * CB + ZB, [P, ZW])
        prob = at("prob", FREE + 5 * CB + 2 * ZB, [P, ZW])
        probT_hi = at("probT_hi", FREE + 5 * CB + 3 * ZB, [P, ZW], f32r)
        probT_lo = at("probT_lo", HB + FREE + 5 * CB, [P, ZW], f32r)
        left = at("left", FREE + 5 * CB + 4 * ZB, [P, ZW + 2])
        vn = at("vn", HB + FREE, [P, RT, D])
        wsT = at("wsT", HB + FREE + RT * D * 4, [P, KD, P])
        ws_raw = at("ws_raw", FREE, [P, KD, P])
        u_s = at("u_s", FREE + KD * P * 4, [P, RT, CH])
        ws_cur = at("ws_cur", FREE + KD * P * 4 + CB, [P, TC, P])

        acc = ctx.enter_context(nc.psum_tensor("acc", [P, 2 * RT * CH], f32))
        tp = [ctx.enter_context(nc.psum_tensor(f"tp{i}", [P, TC * S], f32)) for i in range(2)]

        raw_loaded = [sem(f"raw_loaded{i}") for i in range(RING)]
        hi_ready, lo_ready, used = sem("hi_ready"), sem("lo_ready"), sem("used")
        consts_filled, consts_ready = sem("consts_filled"), sem("consts_ready")
        first_loaded, rows_loaded = sem("first_loaded"), sem("rows_loaded")
        rows_turned, cols_ready = sem("rows_turned"), sem("cols_ready")
        x_loaded = [sem(f"x_loaded{c}") for c in range(ND)]
        n_turned = [sem(f"n{m}_turned") for m in range(4)]
        n_hi = [sem(f"n{m}_hi") for m in range(4)]
        n_lo = [sem(f"n{m}_lo") for m in range(4)]
        n_sq = [sem(f"n{m}_sq") for m in range(5)]
        n_step, n_total, n_rstd = ({m: sem(f"n{m}_{what}") for m in (0, 1, 2, 3, 5)}
                                   for what in ("step", "total", "rstd"))
        q_out, k_out, v_high, v_out = sem("q_out"), sem("k_out"), sem("v_high"), sem("v_out")
        qk_turned, qkT_high, qkT_ready = sem("qk_turned"), sem("qkT_high"), sem("qkT_ready")
        z_ready, sig_ready = sem("z_ready"), sem("sig_ready")
        scan_ready, prod_ready, prob_ready = sem("scan_ready"), sem("prod_ready"), sem("prob_ready")
        pT_turned, pT_high, pT_ready = sem("pT_turned"), sem("pT_high"), sem("pT_ready")
        o_ready, o_hi, o_lo = sem("o_ready"), sem("o_hi"), sem("o_lo")
        res_ready = [sem(f"res_ready{i}") for i in range(4)]
        spread_ready = [sem(f"spread_ready{i}") for i in range(2)]
        row_out = [sem(f"row_out{i}") for i in range(2)]
        row_ready = [sem(f"row_ready{i}") for i in range(2)]
        gate_low = [sem(f"gate_low{i}") for i in range(2)]
        up_low = [sem(f"up_low{i}") for i in range(2)]
        gate_summed = [sem(f"gate_summed{i}") for i in range(2)]
        gate_scaled = [sem(f"gate_scaled{i}") for i in range(2)]
        gate_ready = [sem(f"gate_ready{i}") for i in range(2)]
        up_summed = [sem(f"up_summed{i}") for i in range(2)]
        up_scaled = [sem(f"up_scaled{i}") for i in range(2)]
        f_res = [sem(f"f_res{i}") for i in range(2)]
        f_hi = [sem(f"f_hi{i}") for i in range(2)]
        f_lo = [sem(f"f_lo{i}") for i in range(2)]
        vgain_loaded, fgain_loaded, ws_loaded = sem("vgain_loaded"), sem("fgain_loaded"), sem("ws_loaded")
        ws_turned, wsT_ready, gelu_ready, stats_ready = (sem("ws_turned"), sem("wsT_ready"), sem("gelu_ready"),
                                                         sem("stats_ready"))
        vn_step, vn_ready, ws_cur_ready, mixed_ready = (sem("vn_step"), sem("vn_ready"), sem("ws_cur_ready"),
                                                        sem("mixed_ready"))
        y_ready, y_turned, y_hi, y_lo = sem("y_ready"), sem("y_turned"), sem("y_hi"), sem("y_lo")
        first_rows = sem("first_rows")
        gained, total_r = sem("gained"), [sem("total_r0"), sem("total_r1")]
        step_r, rstd_r = [sem("step_r0"), sem("step_r1")], [sem("rstd_r0"), sem("rstd_r1")]
        out_r0, out_act, out_dve, stored = sem("out_r0"), sem("out_act"), sem("out_dve"), sem("stored")

        block = ctx.enter_context(nc.Block())

        def fills(base, it, per, p):
            return base // RING + it * (per // RING) + p // RING + 1

        def acc_at(chunk, rt):
            return acc[:, bass.ds(half(chunk) * (RT * CH) + rt * CH, CH)]

        def acc_both(chunk):
            return acc[:, bass.ds(half(chunk) * (RT * CH), RT * CH)].rearrange("p (r n) -> p r n", r=RT)

        GATE_BANKS = (acc[:, 0:RT * CH], tp[1][:, :])
        UP_BANKS = (acc[:, RT * CH:2 * RT * CH], tp[0][:, :])

        def parts(bank_pair, which):
            return bank_pair.rearrange("p (k v t) -> p k v t", k=2, v=2)[:, :, which]

        def tile(t, k):
            return t[:, bass.ds(k, 1), :].rearrange("p k t -> p (k t)")

        @block.sync
        def _(sp):
            def load_x(c):
                sp.dma_start(h[:, :, c * CH:(c + 1) * CH],
                             x[:, c * CH:(c + 1) * CH].rearrange("(r p) n -> p r n", p=P)).then_inc(x_loaded[c], 16)

            def load(base, it, per, p, src, k0):
                if not (base == 0 and isinstance(it, int) and it == 0 and p < RING):
                    sp.wait_ge(lo_ready, base + it * per + p - RING + 1)
                sp.dma_start(raw[:, p % RING], src[:, k0:k0 + KP, :]).then_inc(raw_loaded[p % RING], 16)

            qkv = sb_w_qkv[0].rearrange("(k p) n -> p k n", p=P)

            def qkv_body(j, first):
                for sec in range(3):
                    src = qkv[:, :, bass.ds(j * CH + sec * D, CH)]
                    for p in range(PD):
                        if first and sec == 0 and p < ND:
                            load_x(p)
                        load(AT_QKV, j, 3 * PD, sec * PD + p, src, p * KP)

            def square(base, w):
                src = w.rearrange("(k p) n -> p k n", p=P)
                with sp.Fori(0, w.shape[1] // CH) as c:
                    for p in range(PD):
                        load(base, c, PD, p, src[:, :, bass.ds(c * CH, CH)], p * KP)

            def ffn(layer):
                up = ffn_w_gate_up[layer].rearrange("(k p) n -> p k n", p=P)
                with sp.Fori(0, NF) as i:
                    for sec in range(2):
                        src = up[:, :, bass.ds(i * CH + sec * F, CH)]
                        for p in range(PD):
                            load(AT_UP[layer], i, 2 * PD, sec * PD + p, src, p * KP)
                down = ffn_w_down[layer].rearrange("(k p) n -> p k n", p=P)
                with sp.Fori(0, ND // 2) as i:
                    for cc in range(2):
                        src = down[:, :, bass.ds(i * (2 * CH) + cc * CH, CH)]
                        for p in range(PF):
                            load(AT_DOWN[layer], i, 2 * PF, cc * PF + p, src, p * KP)

            qkv_body(0, True)
            with sp.Fori(1, ND) as j:
                qkv_body(j, False)
            square(AT_SBO, sb_w_o[0])
            ffn(0)
            w_in = gm_w_in[0].rearrange("(k p) n -> p k n", p=P)
            for sec in range(2):
                with sp.Fori(0, ND) as c:
                    for p in range(PD):
                        load(AT_GMI + sec * ND * PD, c, PD, p, w_in[:, :, bass.ds(c * CH + (1 - sec) * D, CH)], p * KP)
            square(AT_GMO, gm_w_o[0])
            ffn(1)
            o = out.rearrange("(r p) n -> p r n", p=P)
            for done, r, cs in ((out_r0, 0, slice(0, D)), (out_dve, 1, slice(0, D // 2)),
                                (out_act, 1, slice(D // 2, D))):
                sp.wait_ge(done, 1)
                sp.dma_start(o[:, r, cs], h[:, r, cs]).then_inc(stored, 16)
            sp.wait_ge(stored, 16 * 3)

        @block.gpsimd
        def _(pool):
            for t, v in ((ident[:, :], 0.0), (below[:, :], 1.0), (upto[:, :], 1.0), (stop[:, :], 1.0),
                         (minus_half[:, :], -0.5), (left[:, ZW:ZW + 2], 1.0)):
                nc.gpsimd.memset(t, v).then_inc(consts_filled, 1)
            pool.wait_ge(consts_filled, 6)

            def select(t, op, fill, base, pattern, mul):
                return nc.gpsimd.affine_select(out=t, in_=t, compare_op=op, fill=fill, base=base, pattern=pattern,
                                               channel_multiplier=mul)

            select(ident[:, :], ALU.not_equal, 1.0, 0, [[-1, P]], 1).then_inc(consts_ready, 1)
            select(below[:, :], ALU.is_gt, 0.0, 0, [[-1, P]], 1).then_inc(consts_ready, 1)
            select(upto[:, :], ALU.is_ge, 0.0, 0, [[1, P]], -1).then_inc(consts_ready, 1)
            select(stop[:, 0:P], ALU.is_ge, 0.0, 0, [[1, P]], -1).then_inc(consts_ready, 1)
            select(stop[:, P:3 * P], ALU.is_ge, 0.0, -P, [[1, 2 * P]], -1).then_inc(consts_ready, 1)

            for m, src in enumerate((ffn_norm[0], gm_norm[0], ffn_norm[1])):
                nc.gpsimd.dma_start(rows[m * KD:(m + 1) * KD, :],
                                    src.rearrange("(k p) -> k p", p=P)).then_inc(rows_loaded, 16)
            nc.gpsimd.dma_start(rows[3 * KD:4 * KD, :], gm_b_s[0]).then_inc(rows_loaded, 16)

            def power(m):
                pool.wait_ge(n_total[m], 1)
                nc.gpsimd.tensor_tensor(out=rstd[:, m, :], in0=total[:, m, :], in1=minus_half[:, :],
                                        op=ALU.pow).then_inc(n_rstd[m], 1)

            power(0)
            nc.gpsimd.dma_start(gain_bc[:, :], gm_v_norm[0:1, :].to_broadcast([P, D])).then_inc(vgain_loaded, 16)
            power(1)
            pool.wait_ge(used, AT_GMI)
            nc.gpsimd.dma_start(ws_raw[:, :, :], gm_w_s[0].rearrange("g t s -> t g s")).then_inc(ws_loaded, 16)
            power(2)
            power(5)
            pool.wait_ge(vn_ready, RT)
            nc.gpsimd.dma_start(gain_bc[:, :], final_norm[0:1, :].to_broadcast([P, D])).then_inc(fgain_loaded, 16)
            power(3)
            for r in range(RT):
                pool.wait_ge(total_r[r], 1)
                nc.gpsimd.tensor_tensor(out=rstd[:, 4, r:r + 1], in0=total[:, 4, r:r + 1],
                                        in1=minus_half[:, r:r + 1], op=ALU.pow).then_inc(rstd_r[r], 1)

        @block.scalar
        def _(act):
            act.dma_start(rows_first[:, :], sb_norm[0].rearrange("(k p) -> k p", p=P)).then_inc(first_loaded, 16)

            def split(base, it, per, p):
                act.wait_ge(raw_loaded[p % RING], 16 * fills(base, it, per, p))
                if not (base == 0 and isinstance(it, int) and it == 0 and p < RING):
                    act.wait_ge(used, base + it * per + p - RING + 1)
                nc.scalar.activation(w_hi[:, p % RING], raw[:, p % RING], ACT.Copy).then_inc(hi_ready, 1)

            def ahead(base, it, per, p):
                if not (base == AT_DOWN[1] and isinstance(it, int) and base + it * per + p + LEAD >= PIECES):
                    split(base, it, per, p + LEAD)

            def turned_gained(m, c, seen):
                act.wait_ge(n_turned[m], seen)
                for k in range(TC):
                    last = nc.scalar.activation(tile(xT_hi, c * TC + k),
                                                tp[0 if m or half(c) == 0 else 1][:, k * S:(k + 1) * S], ACT.Copy,
                                                scale=cols[:, bass.ds(c * TC + (m * KD + k), 1)])
                last.then_inc(n_hi[m], 1)

            def squares(m, c, src):
                for r in range(RT):
                    last = nc.scalar.activation(junk[:, r], src[:, r], ACT.Square,
                                                accum_out=sumsq[:, m, r, bass.ds(c, 1)])
                last.then_inc(n_sq[m], 1)

            def norm_chunk(m, c):
                turned_gained(m, c, c + 1)
                nc.scalar.activation(h[:, :, bass.ds(c * CH, CH)], res[:, :, :], ACT.Copy)
                squares(m, c, res)

            def q_or_k(j, sec, dst, done, t_end):
                act.wait_ge(used, AT_QKV + j * (3 * PD) + t_end)
                for r in range(RT):
                    last = nc.scalar.activation(dst[:, r], acc_at(j * 3 + sec, r), ACT.Copy, scale=rstd[:, 0, r:r + 1])
                last.then_inc(done, 1)

            def qkT_highs(g, second):
                act.wait_ge(qk_turned, g * 2 + (1 + second))
                dst = kT_hi if second else qT_hi
                nc.scalar.activation(dst[:, :, :], tp[second][:, :].rearrange("p (h t) -> p h t", h=HG),
                                     ACT.Copy).then_inc(qkT_high, 1)

            def v_highs(j):
                act.wait_ge(used, AT_QKV + j * (3 * PD) + 3 * PD)
                for r in range(RT):
                    last = nc.scalar.activation(v_hi[:, r], acc_at(j * 3 + 2, r), ACT.Copy, scale=rstd[:, 0, r:r + 1])
                last.then_inc(v_high, 1)

            def sigmoids(g, i):
                act.wait_ge(z_ready, g * HG + (i + 1))
                nc.scalar.activation(keep[:, :], tp[0][:, 0:ZW], ACT.Sigmoid, scale=-SB_SCALE)
                nc.scalar.activation(take[:, :], tp[0][:, 0:ZW], ACT.Sigmoid, scale=SB_SCALE).then_inc(sig_ready, 1)

            def probT_high(g, i):
                act.wait_ge(pT_turned, g * HG + (i + 1))
                nc.scalar.activation(probT_hi[:, :], tp[0][:, CH:CH + ZW], ACT.Copy).then_inc(pT_high, 1)

            def o_high(g, i):
                act.wait_ge(o_ready, g * HG + (i + 1))
                nc.scalar.activation(tile(hid_hi, g * HG + i), tp[1][:, (i % 2) * CH:(i % 2) * CH + S],
                                     ACT.Copy).then_inc(o_hi, 1)

            def attention(g, t):
                if t == 1:
                    qkT_highs(g, 0)
                if t == 3:
                    qkT_highs(g, 1)
                for i in range(HG):
                    if t == 9 + 4 * i:
                        o_high(g, i)
                    if t == 7 + 4 * i:
                        probT_high(g, i)
                for i in range(HG):
                    if t == 5 + 4 * i:
                        sigmoids(g, i)

            split(AT_QKV, 0, 3 * PD, 0)
            act.wait_ge(rows_turned, 1)
            nc.scalar.activation(cols[:, 0:KD], tp[1][:, 0:KD], ACT.Copy).then_inc(cols_ready, 1)
            act.wait_ge(cols_ready, 1)
            turned_gained(0, 0, 1)
            split(AT_QKV, 0, 3 * PD, 1)
            turned_gained(0, 1, 2)
            split(AT_QKV, 0, 3 * PD, 2)

            def qkv_round(j, with_attention):
                for t in range(3 * PD):
                    ahead(AT_QKV, j, 3 * PD, t)
                    if not with_attention:
                        if t < 2:
                            turned_gained(0, 2 + t, 3 + t)
                        elif t < 2 + ND:
                            c = t - 2
                            if c:
                                act.wait_ge(n_sq[0], c)
                            squares(0, c, h[:, :, c * CH:(c + 1) * CH])
                        if t == 6:
                            act.wait_ge(rows_turned, 2)
                            nc.scalar.activation(cols[:, KD:5 * KD], tp[0][:, 0:4 * KD],
                                                 ACT.Copy).then_inc(cols_ready, 1)
                    if t == PD - 1:
                        if not with_attention:
                            act.wait_ge(n_rstd[0], 1)
                        q_or_k(j, 0, q_s, q_out, PD)
                    if t == 2 * PD - 1:
                        q_or_k(j, 1, k_s, k_out, 2 * PD)
                    if t == 3 * PD - 1:
                        v_highs(j)
                    if with_attention:
                        attention(j - 1, t)

            qkv_round(0, False)
            with act.Fori(1, ND) as j:
                qkv_round(j, True)
            g = ND - 1
            for p in range(PD):
                ahead(AT_SBO, 0, PD, p)
                if p == 0:
                    qkT_highs(g, 0)
                    qkT_highs(g, 1)
                for i in range(HG):
                    if p == 3 + i:
                        o_high(g, i)
                    if p == 2 + i:
                        probT_high(g, i)
                for i in range(HG):
                    if p == 1 + i:
                        sigmoids(g, i)

            def residual_rest(m, base):
                with act.Fori(1, ND) as c:
                    for p in range(PD):
                        ahead(base, c, PD, p)
                        if p == 1:
                            norm_chunk(m, c - 1)

            residual_rest(1, AT_SBO)

            def rstd_row_out(layer):
                act.wait_ge(row_out[layer], 1)
                nc.scalar.activation(rstd_row[:, :], UP_BANKS[0][:, 0:S], ACT.Copy).then_inc(row_ready[layer], 1)

            def low_out(layer, dst, banks, t_end, done):
                act.wait_ge(used, AT_UP[layer] + t_end)
                for n in range(2):
                    last = nc.scalar.activation(dst[:, 2 * n:2 * n + 2, :], parts(banks[n], 1), ACT.Copy)
                last.then_inc(done[layer], 1)

            def gate_silu(layer, i):
                act.wait_ge(gate_scaled[layer], i + 1)
                nc.scalar.activation(gate[:, :, :], gate[:, :, :], ACT.Silu).then_inc(gate_ready[layer], 1)

            def hidden_high(layer, i):
                act.wait_ge(f_res[layer], i + 1)
                nc.scalar.activation(hid_hi[:, bass.ds(i * TC, TC), :], hidden, ACT.Copy).then_inc(f_hi[layer], 1)

            def ffn_up(layer):
                m = 1 + 2 * layer
                for p in range(PD):
                    ahead(AT_UP[layer], 0, PD, p)
                    if p == 1:
                        norm_chunk(m, ND - 1)
                    if p == PD - 2:
                        rstd_row_out(layer)
                    if p == PD - 1:
                        low_out(layer, gate, GATE_BANKS, PD, gate_low)
                with act.Fori(0, NF - 1) as i:
                    for t in range(2 * PD):
                        ahead(AT_UP[layer] + PD, i, 2 * PD, t)
                        if t == 0:
                            gate_silu(layer, i)
                        if t == PD - 1:
                            low_out(layer, hidden, UP_BANKS, i * (2 * PD) + 2 * PD, up_low)
                        if t == PD + 1:
                            hidden_high(layer, i)
                        if t == 2 * PD - 1:
                            low_out(layer, gate, GATE_BANKS, i * (2 * PD) + 3 * PD, gate_low)
                            act.wait_ge(f_lo[layer], i + 1)
                for p in range(PD):
                    ahead(AT_UP[layer] + (2 * NF - 1) * PD, 0, PD, p)
                    if p == 0:
                        gate_silu(layer, NF - 1)
                low_out(layer, hidden, UP_BANKS, 2 * NF * PD, up_low)

            ffn_up(0)
            for it in range(ND // 2):
                for t in range(2 * PF):
                    ahead(AT_DOWN[0], it, 2 * PF, t)
                    if t == 1 and it == 0:
                        hidden_high(0, NF - 1)
                    if t == 1 and it > 0:
                        norm_chunk(2, 2 * it - 1)
                    if t == PF + 1:
                        norm_chunk(2, 2 * it)

            def gelu(c, dst):
                act.wait_ge(used, AT_GMI + PD + c * PD)
                for r in range(RT):
                    last = nc.scalar.activation(dst[r], acc_at(c, r), ACT.Gelu_apprx_tanh, scale=rstd[:, 2, r:r + 1])
                last.then_inc(gelu_ready, 1)

            def ws_evac(n):
                act.wait_ge(ws_turned, n + 1)
                nc.scalar.activation(wsT[:, n * 8:(n + 1) * 8, :], tp[1][:, :].rearrange("p (g t) -> p g t", g=8),
                                     ACT.Copy).then_inc(wsT_ready, 1)

            for p in range(PD):
                ahead(AT_GMI, 0, PD, p)
                if p == 1:
                    norm_chunk(2, ND - 1)
                if p == 5:
                    ws_evac(0)
                if p == 7:
                    act.wait_ge(n_rstd[2], 1)
                    gelu(0, [vn[:, r, 0:CH] for r in range(RT)])
                    ws_evac(1)
            with act.Fori(1, ND) as c:
                for p in range(PD):
                    ahead(AT_GMI, c, PD, p)
                    if p == PD - 1:
                        gelu(c, [vn[:, r, bass.ds(c * CH, CH)] for r in range(RT)])

            def y_high(c):
                act.wait_ge(y_turned, c + 1)
                nc.scalar.activation(hid_hi[:, bass.ds(c * TC, TC), :],
                                     tp[0][:, :].rearrange("p (k t) -> p k t", k=TC), ACT.Copy).then_inc(y_hi, 1)

            def u_chunk(c, carried):
                for p in range(PD):
                    ahead(AT_GMI + ND * PD, c, PD, p)
                    if p == 1 and carried:
                        y_high(c - 1)
                    if p == PD - 1:
                        gelu(c + ND, [u_s[:, r] for r in range(RT)])

            u_chunk(0, False)
            with act.Fori(1, ND) as c:
                u_chunk(c, True)
            for p in range(PD):
                ahead(AT_GMO, 0, PD, p)
                if p == 1:
                    y_high(ND - 1)
            residual_rest(3, AT_GMO)
            ffn_up(1)

            def final_squares(c):
                act.wait_ge(res_ready[3], c + 2)
                squares(4, c, h[:, :, c * CH:(c + 1) * CH])

            def last_squares():
                for r in range(RT):
                    act.wait_ge(res_ready[3], ND + 1 + r)
                    nc.scalar.activation(junk[:, r], h[:, r, (ND - 1) * CH:ND * CH], ACT.Square,
                                         accum_out=sumsq[:, 4, r, ND - 1:ND]).then_inc(n_sq[4], 1)

            for it in range(ND // 2):
                for t in range(2 * PF):
                    ahead(AT_DOWN[1], it, 2 * PF, t)
                    if t == 1 and it == 0:
                        hidden_high(1, NF - 1)
                    if t == PF - 1:
                        final_squares(2 * it)
                    if t == 2 * PF - 1:
                        if it == 0:
                            final_squares(1)
                        else:
                            last_squares()
            act.wait_ge(rstd_r[1], 1)
            act.wait_ge(gained, ND + 1)
            nc.scalar.activation(h[:, 1, D // 2:], h[:, 1, D // 2:], ACT.Copy, scale=rstd[:, 4, 1:2]).then_inc(out_act, 1)

        @block.vector
        def _(dve):
            def split(base, it, per, p):
                dve.wait_ge(hi_ready, base + it * per + p + 1)
                nc.vector.tensor_tensor(w_lo[:, p % RING], raw[:, p % RING], w_hi[:, p % RING].bitcast(f32),
                                        ALU.subtract).then_inc(lo_ready, 1)

            def ahead(base, it, per, p):
                if not (base == AT_DOWN[1] and isinstance(it, int) and base + it * per + p + LEAD >= PIECES):
                    split(base, it, per, p + LEAD)

            def gained_low(m, c, seen):
                dve.wait_ge(n_hi[m], seen)
                for k in range(TC):
                    last = nc.vector.scalar_tensor_tensor(
                        out=tile(xT_lo, c * TC + k), in0=tp[0 if m or half(c) == 0 else 1][:, k * S:(k + 1) * S],
                        scalar=cols[:, bass.ds(c * TC + (m * KD + k), 1)], in1=tile(xT_hi, c * TC + k).bitcast(f32),
                        op0=ALU.mult, op1=ALU.subtract)
                last.then_inc(n_lo[m], 1)

            def mean_square(m, seen):
                dve.wait_ge(n_sq[m], seen)
                nc.vector.tensor_reduce(out=total[:, m, :], in_=sumsq[:, m], op=ALU.add, axis=AX.X).then_inc(n_step[m], 1)
                dve.wait_ge(n_step[m], 1)
                nc.vector.tensor_scalar(total[:, m, :], total[:, m, :], 1.0 / D, EPS, ALU.mult,
                                        ALU.add).then_inc(n_total[m], 1)

            def add_residual(which, chunk, seen, dst):
                dve.wait_ge(used, seen)
                nc.vector.tensor_tensor(dst, acc_both(chunk), h[:, :, bass.ds(chunk * CH, CH)],
                                        ALU.add).then_inc(res_ready[which], 1)

            def v_lows(j):
                dve.wait_ge(v_high, j + 1)
                for r in range(RT):
                    last = nc.vector.scalar_tensor_tensor(out=v_lo[:, r], in0=acc_at(j * 3 + 2, r),
                                                          scalar=rstd[:, 0, r:r + 1], in1=v_hi[:, r].bitcast(f32),
                                                          op0=ALU.mult, op1=ALU.subtract)
                last.then_inc(v_out, 1)

            def qkT_lows(g, second):
                dve.wait_ge(qkT_high, g * 2 + (1 + second))
                dst, high = (kT_lo, kT_hi) if second else (qT_lo, qT_hi)
                nc.vector.tensor_tensor(dst[:, :, :], tp[second][:, :].rearrange("p (h t) -> p h t", h=HG),
                                        high[:, :, :].bitcast(f32), ALU.subtract).then_inc(qkT_ready, 1)

            def probT_lows(g, i):
                dve.wait_ge(pT_high, g * HG + (i + 1))
                nc.vector.tensor_tensor(probT_lo[:, :], tp[0][:, CH:CH + ZW], probT_hi[:, :].bitcast(f32),
                                        ALU.subtract).then_inc(pT_ready, 1)

            def break_stick(g, i):
                n = g * HG + (i + 1)
                dve.wait_ge(sig_ready, n)
                nc.vector.tensor_tensor_scan(left[:, ZW - 1::-1], keep[:, ZW - 1::-1], stop[:, ZW - 1::-1], 1.0,
                                             ALU.mult, ALU.max).then_inc(scan_ready, 1)
                dve.wait_ge(scan_ready, n)
                nc.vector.tensor_tensor(prob[:, :], take[:, :], left[:, 1:ZW + 1], ALU.mult).then_inc(prod_ready, 1)
                dve.wait_ge(prod_ready, n)
                for b in (0, 2):
                    last = nc.vector.tensor_tensor(prob[:, b * P:(b + 1) * P], prob[:, b * P:(b + 1) * P], below[:, :],
                                                   ALU.mult)
                last.then_inc(prob_ready, 1)

            def o_low(g, i):
                dve.wait_ge(o_hi, g * HG + (i + 1))
                nc.vector.tensor_tensor(tile(hid_lo, g * HG + i), tp[1][:, (i % 2) * CH:(i % 2) * CH + S],
                                        tile(hid_hi, g * HG + i).bitcast(f32), ALU.subtract).then_inc(o_lo, 1)

            def attention(g, t):
                if t == 1:
                    qkT_lows(g, 0)
                if t == 3:
                    qkT_lows(g, 1)
                for i in range(HG):
                    if t == 9 + 4 * i:
                        o_low(g, i)
                    if t == 7 + 4 * i:
                        probT_lows(g, i)
                for i in range(HG):
                    if t == 5 + 4 * i:
                        break_stick(g, i)

            split(AT_QKV, 0, 3 * PD, 0)
            dve.wait_ge(cols_ready, 1)
            gained_low(0, 0, 1)
            split(AT_QKV, 0, 3 * PD, 1)
            gained_low(0, 1, 2)
            split(AT_QKV, 0, 3 * PD, 2)
            dve.wait_ge(consts_ready, 5)

            def qkv_round(j, with_attention):
                for t in range(3 * PD):
                    ahead(AT_QKV, j, 3 * PD, t)
                    if t < 2 and not with_attention:
                        gained_low(0, 2 + t, 3 + t)
                    if t == 6 and not with_attention:
                        mean_square(0, ND)
                    if with_attention:
                        attention(j - 1, t)
                    if t == 3 * PD - 1:
                        if not with_attention:
                            dve.wait_ge(n_rstd[0], 1)
                        v_lows(j)

            qkv_round(0, False)
            with dve.Fori(1, ND) as j:
                qkv_round(j, True)
            g = ND - 1
            for p in range(PD):
                ahead(AT_SBO, 0, PD, p)
                if p == 0:
                    qkT_lows(g, 0)
                    qkT_lows(g, 1)
                for i in range(HG):
                    if p == 3 + i:
                        o_low(g, i)
                    if p == 2 + i:
                        probT_lows(g, i)
                for i in range(HG):
                    if p == 1 + i:
                        break_stick(g, i)
                if p == PD - 1:
                    add_residual(0, 0, AT_SBO + PD, res[:, :, :])

            def residual_rest(which, m, base):
                with dve.Fori(1, ND) as c:
                    for p in range(PD):
                        ahead(base, c, PD, p)
                        if p == 1:
                            gained_low(m, c - 1, c)
                        if p == PD - 1:
                            dve.wait_ge(n_sq[m], c)
                            add_residual(which, c, base + PD + c * PD, res[:, :, :])

            residual_rest(0, 1, AT_SBO)

            def rstd_spread(layer):
                m = 1 + 2 * layer
                dve.wait_ge(n_rstd[m], 1)
                for r in range(RT):
                    last = nc.vector.tensor_scalar(spread[:, r], ident[:, :], 0.0, rstd[:, m, r:r + 1], ALU.mult,
                                                   ALU.add)
                last.then_inc(spread_ready[layer], 1)

            def add_high(dst, banks, done):
                for n in range(2):
                    part = dst[:, 2 * n:2 * n + 2, :]
                    last = nc.vector.tensor_tensor(part, parts(banks[n], 0), part, ALU.add)
                last.then_inc(done, 1)

            def by_rstd(t, done):
                nc.vector.tensor_tensor(t, t, rstd_row[:, :].unsqueeze(1).to_broadcast([P, TC, S]),
                                        ALU.mult).then_inc(done, 1)

            def gate_out(layer, i):
                dve.wait_ge(gate_low[layer], i + 1)
                add_high(gate, GATE_BANKS, gate_summed[layer])
                dve.wait_ge(gate_summed[layer], i + 1)
                by_rstd(gate[:, :, :], gate_scaled[layer])

            def up_out(layer, i, read, seen):
                dve.wait_ge(up_low[layer], i + 1)
                add_high(hidden, UP_BANKS, read)
                dve.wait_ge(read, seen)
                by_rstd(hidden, up_scaled[layer])
                dve.wait_ge(gate_ready[layer], i + 1)
                dve.wait_ge(up_scaled[layer], i + 1)
                nc.vector.tensor_tensor(hidden, hidden, gate[:, :, :], ALU.mult).then_inc(f_res[layer], 1)

            def hidden_low(layer, i):
                dve.wait_ge(f_hi[layer], i + 1)
                ks = bass.ds(i * TC, TC)
                nc.vector.tensor_tensor(hid_lo[:, ks, :], hidden, hid_hi[:, ks, :].bitcast(f32),
                                        ALU.subtract).then_inc(f_lo[layer], 1)

            def ffn_up(layer):
                m = 1 + 2 * layer
                for p in range(PD):
                    ahead(AT_UP[layer], 0, PD, p)
                    if p == 1:
                        gained_low(m, ND - 1, ND)
                    if p == 2:
                        mean_square(m, ND)
                    if p == 3:
                        rstd_spread(layer)
                    if p == PD - 1:
                        dve.wait_ge(row_ready[layer], 1)
                        gate_out(layer, 0)
                with dve.Fori(0, NF - 1) as i:
                    for t in range(2 * PD):
                        ahead(AT_UP[layer] + PD, i, 2 * PD, t)
                        if t == PD - 1:
                            up_out(layer, i, up_summed[layer], i + 1)
                        if t == PD + 1:
                            hidden_low(layer, i)
                        if t == 2 * PD - 1:
                            gate_out(layer, i + 1)
                for p in range(PD):
                    ahead(AT_UP[layer] + (2 * NF - 1) * PD, 0, PD, p)
                up_out(layer, NF - 1, res_ready[1 + 2 * layer], 1)

            ffn_up(0)
            for it in range(ND // 2):
                for t in range(2 * PF):
                    c = 2 * it + t // PF
                    ahead(AT_DOWN[0], it, 2 * PF, t)
                    if t == 1 and it == 0:
                        hidden_low(0, NF - 1)
                    elif t % PF == 1:
                        gained_low(2, c - 1, c)
                    if t % PF == PF - 1:
                        if c:
                            dve.wait_ge(n_sq[2], c)
                        add_residual(1, c, AT_DOWN[0] + (c + 1) * PF, res[:, :, :])

            def v_stats(c):
                dve.wait_ge(gelu_ready, c + 1)
                for r in range(RT):
                    last = nc.vector.bn_stats(tile(stats[:, r], c), vn[:, r, bass.ds(c * CH, CH)])
                last.then_inc(stats_ready, 1)

            for p in range(PD):
                ahead(AT_GMI, 0, PD, p)
                if p == 1:
                    gained_low(2, ND - 1, ND)
                if p == 2:
                    mean_square(2, ND)
                if p == PD - 1:
                    v_stats(0)
            with dve.Fori(1, ND) as c:
                for p in range(PD):
                    ahead(AT_GMI, c, PD, p)
                    if p == PD - 1:
                        v_stats(c)

            def norm_v(r):
                dve.wait_ge(n_rstd[5], 1)
                nc.vector.tensor_scalar(vn[:, r], vn[:, r], moments[:, r, 0:1], rstd[:, 5, r:r + 1], ALU.subtract,
                                        ALU.mult).then_inc(vn_step, 1)
                dve.wait_ge(vn_step, r + 1)
                nc.vector.tensor_tensor(vn[:, r], vn[:, r], gain_bc[:, :], ALU.mult).then_inc(vn_ready, 1)

            def ws_mask(c):
                for g in range(TC):
                    last = nc.vector.tensor_tensor(ws_cur[:, g], tile(wsT, c * TC + g), upto[:, :], ALU.mult)
                last.then_inc(ws_cur_ready, 1)

            def gated(c):
                dve.wait_ge(mixed_ready, c + 1)
                dve.wait_ge(gelu_ready, c + (ND + 1))
                for r in range(RT):
                    for g in range(TC):
                        cs = slice(g * P, (g + 1) * P)
                        last = nc.vector.scalar_tensor_tensor(
                            out=res[:, r, cs], in0=tp[1][:, r * CH + g * P:r * CH + (g + 1) * P],
                            scalar=cols[:, bass.ds(c * TC + (4 * KD + g), 1)], in1=u_s[:, r, cs],
                            op0=ALU.add, op1=ALU.mult)
                last.then_inc(y_ready, 1)

            def y_low(c):
                dve.wait_ge(y_hi, c + 1)
                ks = bass.ds(c * TC, TC)
                nc.vector.tensor_tensor(hid_lo[:, ks, :], tp[0][:, :].rearrange("p (k t) -> p k t", k=TC),
                                        hid_hi[:, ks, :].bitcast(f32), ALU.subtract).then_inc(y_lo, 1)

            dve.wait_ge(stats_ready, ND)
            for r in range(RT):
                last = nc.vector.bn_aggr(moments[:, r], stats[:, r].rearrange("p c s -> p (c s)"))
            last.then_inc(n_step[5], 1)
            dve.wait_ge(n_step[5], 1)
            nc.vector.tensor_scalar(total[:, 5, :], moments[:, :, 1], EPS, None, ALU.add).then_inc(n_total[5], 1)
            for p in range(PD):
                ahead(AT_GMI + ND * PD, 0, PD, p)
                if p == 1:
                    dve.wait_ge(wsT_ready, 2)
                    ws_mask(0)
                    dve.wait_ge(vgain_loaded, 16)
                    norm_v(0)
                if p == 3:
                    norm_v(1)
                if p == PD - 1:
                    gated(0)
            with dve.Fori(1, ND) as c:
                for p in range(PD):
                    ahead(AT_GMI + ND * PD, c, PD, p)
                    if p == 0:
                        ws_mask(c)
                    if p == 1:
                        y_low(c - 1)
                    if p == PD - 1:
                        gated(c)
            for p in range(PD):
                ahead(AT_GMO, 0, PD, p)
                if p == 1:
                    y_low(ND - 1)
                if p == PD - 1:
                    add_residual(2, 0, AT_GMO + PD, res[:, :, :])
            residual_rest(2, 3, AT_GMO)
            ffn_up(1)
            dve.wait_ge(fgain_loaded, 16)

            def gain_final(c):
                dve.wait_ge(n_sq[4], c + 1)
                for r in range(RT):
                    last = nc.vector.tensor_tensor(h[:, r, c * CH:(c + 1) * CH], h[:, r, c * CH:(c + 1) * CH],
                                                   gain_bc[:, c * CH:(c + 1) * CH], ALU.mult)
                last.then_inc(gained, 1)

            for it in range(ND // 2):
                for t in range(2 * PF):
                    c = 2 * it + t // PF
                    ahead(AT_DOWN[1], it, 2 * PF, t)
                    if t == 1 and it == 0:
                        hidden_low(1, NF - 1)
                    if t % PF == 1 and c:
                        gain_final(c - 1)
                    if t % PF == PF - 1 and c < ND - 1:
                        add_residual(3, c, AT_DOWN[1] + (c + 1) * PF, h[:, :, c * CH:(c + 1) * CH])
            last_cs = slice((ND - 1) * CH, ND * CH)

            def last_add(r):
                nc.vector.tensor_tensor(h[:, r, last_cs], acc_at(ND - 1, r), h[:, r, last_cs],
                                        ALU.add).then_inc(res_ready[3], 1)

            def last_mean_square(r):
                dve.wait_ge(n_sq[4], ND + r)
                nc.vector.tensor_reduce(out=total[:, 4, r:r + 1], in_=sumsq[:, 4, r], op=ALU.add,
                                        axis=AX.X).then_inc(step_r[r], 1)
                dve.wait_ge(step_r[r], 1)
                nc.vector.tensor_scalar(total[:, 4, r:r + 1], total[:, 4, r:r + 1], 1.0 / D, EPS, ALU.mult,
                                        ALU.add).then_inc(total_r[r], 1)
                nc.vector.tensor_tensor(h[:, r, last_cs], h[:, r, last_cs], gain_bc[:, last_cs],
                                        ALU.mult).then_inc(gained, 1)

            dve.wait_ge(first_rows, ND // 2)
            last_add(0)
            last_mean_square(0)
            dve.wait_ge(used, PIECES)
            last_add(1)
            dve.wait_ge(rstd_r[0], 1)
            dve.wait_ge(gained, ND)
            nc.vector.tensor_scalar(h[:, 0], h[:, 0], rstd[:, 4, 0:1], None, ALU.mult).then_inc(out_r0, 1)
            last_mean_square(1)
            dve.wait_ge(rstd_r[1], 1)
            nc.vector.tensor_scalar(h[:, 1, 0:D // 2], h[:, 1, 0:D // 2], rstd[:, 4, 1:2], None,
                                    ALU.mult).then_inc(out_dve, 1)

        @block.tensor
        def _(pe):
            def piece(base, it, per, p, chunk, k0, K, hi, lo):
                pe.wait_ge(lo_ready, base + it * per + p + 1)
                for k in range(KP):
                    kt = k0 + k
                    for r in range(RT):
                        rs = slice(r * P, (r + 1) * P)
                        dst = acc_at(chunk, r)
                        nc.tensor.matmul(dst, hi[:, kt, rs], w_hi[:, p % RING, k], start=(kt == 0), stop=False)
                        nc.tensor.matmul(dst, hi[:, kt, rs], w_lo[:, p % RING, k], start=False, stop=False)
                        last = nc.tensor.matmul(dst, lo[:, kt, rs], w_hi[:, p % RING, k], start=False,
                                                stop=(kt == K - 1))
                last.then_inc(used, 1)

            def turn(dst, src):
                for k in range(TC):
                    for r in range(RT):
                        last = nc.tensor.transpose(dst[:, k * S + r * P:k * S + (r + 1) * P],
                                                   src[:, r, k * P:(k + 1) * P], ident[:, :])
                return last

            def turn_rows(dst, src, n):
                nc.tensor.transpose(dst, src[:, :], ident[0:n, 0:n]).then_inc(rows_turned, 1)

            def turn_x(c):
                pe.wait_ge(x_loaded[c], 16)
                if c == 1:
                    pe.wait_ge(cols_ready, 1)
                if c >= 2:
                    pe.wait_ge(n_lo[0], c - 1)
                turn(tp[c % 2], h[:, :, c * CH:(c + 1) * CH]).then_inc(n_turned[0], 1)

            def turn_qk(g, second):
                if not second:
                    pe.wait_ge(q_out, g + 1)
                    pe.wait_ge(k_out, g + 1)
                    pe.wait_ge(v_out, g + 1)
                turn(tp[second], k_s if second else q_s).then_inc(qk_turned, 1)

            def scores(g, i):
                if i == 0:
                    pe.wait_ge(qkT_ready, g * 2 + 2)
                else:
                    pe.wait_ge(sig_ready, g * HG + i)
                for r in range(RT):
                    keys = (r + 1) * P
                    dst = tp[0][:, r * P:r * P + keys]
                    rs = slice(r * P, (r + 1) * P)
                    nc.tensor.matmul(dst, qT_hi[:, i, rs], kT_hi[:, i, 0:keys], start=True, stop=False)
                    nc.tensor.matmul(dst, qT_hi[:, i, rs], kT_lo[:, i, 0:keys], start=False, stop=False)
                    last = nc.tensor.matmul(dst, qT_lo[:, i, rs], kT_hi[:, i, 0:keys], start=False, stop=True)
                last.then_inc(z_ready, 1)

            def turn_prob(g, i):
                pe.wait_ge(prob_ready, g * HG + (i + 1))
                if i:
                    pe.wait_ge(pT_ready, g * HG + i)
                for b in range(3):
                    last = nc.tensor.transpose(tp[0][:, CH + b * P:CH + (b + 1) * P], prob[:, b * P:(b + 1) * P],
                                               ident[:, :])
                last.then_inc(pT_turned, 1)

            def values(g, i):
                pe.wait_ge(pT_ready, g * HG + (i + 1))
                if i >= 2:
                    pe.wait_ge(o_lo, g * HG + (i - 1))
                o = tp[1][:, (i % 2) * CH:(i % 2) * CH + S]
                hs = slice(i * P, (i + 1) * P)
                for n, (dst, cs) in enumerate(((o, slice(0, 2 * P)), (o[:, P:2 * P], slice(2 * P, 3 * P)))):
                    nc.tensor.matmul(dst, v_hi[:, n, hs], probT_hi[:, cs], start=(n == 0), stop=False)
                    nc.tensor.matmul(dst, v_hi[:, n, hs], probT_lo[:, cs], start=False, stop=False)
                    last = nc.tensor.matmul(dst, v_lo[:, n, hs], probT_hi[:, cs], start=False, stop=(n == 1))
                last.then_inc(o_ready, 1)

            def attention(g, t):
                if t == 1:
                    turn_qk(g, 0)
                if t == 3:
                    turn_qk(g, 1)
                for i in range(HG):
                    if t == 9 + 4 * i:
                        values(g, i)
                    if t == 7 + 4 * i:
                        turn_prob(g, i)
                for i in range(HG):
                    if t == 5 + 4 * i:
                        scores(g, i)

            def qkv_round(j, with_attention):
                for sec in range(3):
                    for p in range(PD):
                        t = sec * PD + p
                        if p == 0 and (with_attention or sec == 2):
                            pe.wait_ge((k_out, v_out, q_out)[sec], j + (1 if sec == 2 else 0))
                        if not with_attention and sec == 0:
                            pe.wait_ge(n_lo[0], p * KP // TC + 1)
                        piece(AT_QKV, j, 3 * PD, t, j * 3 + sec, p * KP, KD, xT_hi, xT_lo)
                        if not with_attention and t < 2:
                            turn_x(2 + t)
                        if not with_attention and t == 5:
                            pe.wait_ge(rows_loaded, 4 * 16)
                            turn_rows(tp[0][:, 0:4 * KD], rows, 4 * KD)
                        if with_attention:
                            attention(j - 1, t)

            pe.wait_ge(consts_ready, 1)
            turn_x(0)
            pe.wait_ge(first_loaded, 16)
            turn_rows(tp[1][:, 0:KD], rows_first, KD)
            turn_x(1)
            qkv_round(0, False)
            with pe.Fori(1, ND) as j:
                qkv_round(j, True)

            g = ND - 1
            pe.wait_ge(k_out, ND)
            for p in range(PD):
                if p * KP >= (ND - 1) * TC:
                    pe.wait_ge(o_lo, p * KP + KP)
                elif p == 0:
                    pe.wait_ge(o_lo, (ND - 1) * HG)
                piece(AT_SBO, 0, PD, p, 0, p * KP, KD, hid_hi, hid_lo)
                if p == 0:
                    turn_qk(g, 0)
                    turn_qk(g, 1)
                for i in range(HG):
                    if p == 3 + i:
                        values(g, i)
                    if p == 2 + i:
                        turn_prob(g, i)
                for i in range(HG):
                    if p == 1 + i:
                        scores(g, i)

            def residual_rest(which, m, base, hi, lo):
                with pe.Fori(1, ND) as c:
                    for p in range(PD):
                        piece(base, c, PD, p, c, p * KP, KD, hi, lo)
                        if p == 1:
                            pe.wait_ge(res_ready[which], c)
                            turn(tp[0], res).then_inc(n_turned[m], 1)

            pe.wait_ge(v_out, ND)
            residual_rest(0, 1, AT_SBO, hid_hi, hid_lo)

            def turned_piece(base, it, per, p, banks):
                pe.wait_ge(lo_ready, base + it * per + p + 1)
                q = p % PD
                for k in range(KP):
                    kt = q * KP + k
                    for n in range(TC):
                        dst = banks[n // 2][:, (n % 2) * CH:(n % 2 + 1) * CH]
                        ns = slice(n * P, (n + 1) * P)
                        nc.tensor.matmul(dst, w_hi[:, p % RING, k, ns], xT[:, kt].rearrange("p v t -> p (v t)"),
                                         start=(kt == 0), stop=False)
                        last = nc.tensor.matmul(dst[:, 0:S], w_lo[:, p % RING, k, ns], xT[:, kt, 0], start=False,
                                                stop=(kt == KD - 1))
                last.then_inc(used, 1)

            def ffn_up(layer, which):
                m = 1 + 2 * layer
                base = AT_UP[layer]
                for p in range(PD):
                    if p == 0:
                        pe.wait_ge(n_lo[m], ND - 1)
                    if p * KP == (ND - 1) * TC:
                        pe.wait_ge(n_lo[m], ND)
                    turned_piece(base, 0, PD, p, GATE_BANKS)
                    if p == 1:
                        pe.wait_ge(res_ready[which], ND)
                        turn(tp[0], res).then_inc(n_turned[m], 1)
                    if p == PD - 3:
                        pe.wait_ge(spread_ready[layer], 1)
                        for r in range(RT):
                            last = nc.tensor.matmul(UP_BANKS[0][:, r * P:(r + 1) * P], spread[:, r], ident[:, :],
                                                    start=True, stop=True)
                        last.then_inc(row_out[layer], 1)
                pe.wait_ge(row_ready[layer], 1)
                with pe.Fori(0, NF - 1) as i:
                    for t in range(PD):
                        turned_piece(base + PD, i, 2 * PD, t, UP_BANKS)
                    pe.wait_ge(gate_summed[layer], i + 1)
                    for t in range(PD, 2 * PD):
                        turned_piece(base + PD, i, 2 * PD, t, GATE_BANKS)
                    pe.wait_ge(up_summed[layer], i + 1)
                for p in range(PD):
                    turned_piece(base + (2 * NF - 1) * PD, 0, PD, p, UP_BANKS)
                pe.wait_ge(gate_summed[layer], NF)
                pe.wait_ge(f_lo[layer], NF - 1)

            ffn_up(0, 0)
            for it in range(ND // 2):
                for t in range(2 * PF):
                    p = t % PF
                    if t == PF - 2 and it == 0:
                        pe.wait_ge(f_lo[0], NF)
                    if t == PF and it == 0:
                        pe.wait_ge(res_ready[1], 1)
                    piece(AT_DOWN[0], it, 2 * PF, t, t // PF, p * KP, KF, hid_hi, hid_lo)
                    if t % PF == 1 and t + it > 1:
                        pe.wait_ge(res_ready[1], it * 2 + t // PF + 1)
                        turn(tp[0], res).then_inc(n_turned[2], 1)

            for p in range(PD):
                if p == 0:
                    pe.wait_ge(n_lo[2], ND - 1)
                if p * KP == (ND - 1) * TC:
                    pe.wait_ge(n_lo[2], ND)
                piece(AT_GMI, 0, PD, p, 0, p * KP, KD, xT_hi, xT_lo)
                if p == 1:
                    pe.wait_ge(res_ready[1], ND + 1)
                    turn(tp[0], res).then_inc(n_turned[2], 1)
                if p in (5, 7):
                    n = (p - 5) // 2
                    pe.wait_ge(ws_loaded, 16)
                    if n:
                        pe.wait_ge(wsT_ready, 1)
                    for g in range(8):
                        last = nc.tensor.transpose(tp[1][:, g * P:(g + 1) * P], ws_raw[:, n * 8 + g, :], ident[:, :])
                    last.then_inc(ws_turned, 1)
            for p in range(PD):
                piece(AT_GMI + PD, 0, PD, p, 1, p * KP, KD, xT_hi, xT_lo)
            with pe.Fori(2, ND) as c:
                pe.wait_ge(gelu_ready, c - 1)
                for p in range(PD):
                    piece(AT_GMI, c, PD, p, c, p * KP, KD, xT_hi, xT_lo)

            def u_chunk(c, carried):
                pe.wait_ge(gelu_ready, c + (ND - 1))
                for p in range(PD):
                    piece(AT_GMI + ND * PD, c, PD, p, c, p * KP, KD, xT_hi, xT_lo)
                    if p == 1 and carried:
                        pe.wait_ge(y_ready, c)
                        turn(tp[0], res).then_inc(y_turned, 1)
                    if p == 6:
                        pe.wait_ge(ws_cur_ready, c + 1)
                        if not carried:
                            pe.wait_ge(vn_ready, RT)
                        for r in range(RT):
                            for g in range(TC):
                                last = nc.tensor.matmul(tp[1][:, r * CH + g * P:r * CH + (g + 1) * P], ws_cur[:, g],
                                                        vn[:, r, bass.ds(c * CH + g * P, P)], start=True, stop=True)
                        last.then_inc(mixed_ready, 1)

            u_chunk(0, False)
            with pe.Fori(1, ND) as c:
                u_chunk(c, True)
            pe.wait_ge(gelu_ready, 2 * ND - 1)
            for p in range(PD):
                if p == 0:
                    pe.wait_ge(y_lo, ND - 1)
                if p * KP == (ND - 1) * TC:
                    pe.wait_ge(y_lo, ND)
                piece(AT_GMO, 0, PD, p, 0, p * KP, KD, hid_hi, hid_lo)
                if p == 1:
                    pe.wait_ge(y_ready, ND)
                    turn(tp[0], res).then_inc(y_turned, 1)
            pe.wait_ge(gelu_ready, 2 * ND)
            residual_rest(2, 3, AT_GMO, hid_hi, hid_lo)
            ffn_up(1, 2)
            with pe.Fori(0, ND // 2) as it:
                for t in range(2 * PF - 2):
                    p = t % PF
                    if t == PF - 2:
                        pe.wait_ge(f_lo[1], NF)
                    if t == PF:
                        pe.wait_ge(res_ready[3], it * 2 + 1)
                    piece(AT_DOWN[1], it, 2 * PF, t, t // PF, p * KP, KF, hid_hi, hid_lo)
                    if t == PF + 2:
                        pe.wait_ge(res_ready[3], it * 2 + 2)
                for r in range(RT):
                    rs = slice(r * P, (r + 1) * P)
                    dst = acc_at(1, r)
                    for t in (2 * PF - 2, 2 * PF - 1):
                        if r == 0:
                            pe.wait_ge(lo_ready, AT_DOWN[1] + it * (2 * PF) + t + 1)
                        for k in range(KP):
                            kt = (t - PF) * KP + k
                            nc.tensor.matmul(dst, hid_hi[:, kt, rs], w_hi[:, t % RING, k], start=False, stop=False)
                            nc.tensor.matmul(dst, hid_hi[:, kt, rs], w_lo[:, t % RING, k], start=False, stop=False)
                            last = nc.tensor.matmul(dst, hid_lo[:, kt, rs], w_hi[:, t % RING, k], start=False,
                                                    stop=(kt == KF - 1))
                        if r == RT - 1:
                            last.then_inc(used, 1)
                    if r == 0:
                        last.then_inc(first_rows, 1)


_INS = ["x", "sb_norm", "sb_w_qkv", "sb_w_o", "gm_norm", "gm_w_in", "gm_v_norm", "gm_w_s", "gm_b_s", "gm_w_o",
        "ffn_norm", "ffn_w_gate_up", "ffn_w_down", "final_norm"]


def kernel(**inputs):
    import numpy as _np
    import concourse.bacc as _bacc
    from concourse import mybir as _mybir
    from concourse.bass_utils import run_bass_kernel_spmd as _run

    nc = _bacc.Bacc("TRN2", target_bir_lowering=False, num_devices=1)
    arrays, args = {}, []
    for name in _INS:
        a = _np.ascontiguousarray(inputs[name])
        if name == "x":
            a = a.reshape(a.shape[1:])
        if name == "final_norm":
            a = a.reshape(1, -1)
        arrays[f"in_{name}"] = a
        args.append(nc.dram_tensor(f"in_{name}", a.shape, _mybir.dt.from_np(a.dtype), kind="ExternalInput").ap())
    rows, width = arrays["in_x"].shape
    out = nc.dram_tensor("out_0", (rows, width), _mybir.dt.float32, kind="ExternalOutput").ap()
    hybrid_trunk(nc, *args, out)
    r = _run(nc, [arrays], core_ids=[0])
    return r.results[0]["out_0"].reshape(1, rows, width)
```
